# Optimizing a Trainium2 kernel written in Bass

```python
import math
import jax, jax.numpy as jnp
from jax import lax
import numpy as np

D_MODEL = 1024
BATCH = 1
SEQ = 256
DEPTH = 2

N_MIXERS = 2
N_HEADS = 4
QK_DIM = D_MODEL // (2 * N_HEADS)
V_DIM = D_MODEL // N_HEADS
CHUNK = 128
GATE_CAP = 15.0
CONV_WIDTH = 3
D_FF = 4 * D_MODEL
EPS = 1e-6
N_MLSTM_LAYERS = (DEPTH + 1) // 2
N_CONV_LAYERS = DEPTH // 2
QK_COLS = N_HEADS * QK_DIM
MLSTM_IN = 2 * QK_COLS + 2 * D_MODEL + 2 * N_HEADS
CONV_IN = 3 * D_MODEL


def rms_norm(x, g):
    xf = x.astype(jnp.float32)
    y = xf * lax.rsqrt(jnp.mean(xf * xf, axis=-1, keepdims=True) + EPS)
    return (y * g.astype(jnp.float32)).astype(x.dtype)

def mlstm_mixer(x, w_in, b_gates, g_hnorm, w_out):
    B_, S, _ = x.shape
    nc = S // CHUNK
    proj = x @ w_in
    q, k, v, o, gates = jnp.split(
        proj, [QK_COLS, 2 * QK_COLS, 2 * QK_COLS + D_MODEL, 2 * QK_COLS + 2 * D_MODEL], axis=-1)
    f32 = jnp.float32
    q = q.astype(f32).reshape(B_, S, N_HEADS, QK_DIM).transpose(0, 2, 1, 3)
    k = (k.astype(f32) * (QK_DIM ** -0.5)).reshape(B_, S, N_HEADS, QK_DIM).transpose(0, 2, 1, 3)
    v = v.astype(f32).reshape(B_, S, N_HEADS, V_DIM).transpose(0, 2, 1, 3)
    gates = gates.astype(f32) + b_gates.astype(f32)
    gates = GATE_CAP * jnp.tanh(gates / GATE_CAP)
    ig = gates[..., :N_HEADS].transpose(0, 2, 1)
    logf = jax.nn.log_sigmoid(gates[..., N_HEADS:]).transpose(0, 2, 1)

    qc = q.reshape(B_, N_HEADS, nc, CHUNK, QK_DIM)
    kc = k.reshape(B_, N_HEADS, nc, CHUNK, QK_DIM)
    vc = v.reshape(B_, N_HEADS, nc, CHUNK, V_DIM)
    igc = ig.reshape(B_, N_HEADS, nc, CHUNK)
    bcum = jnp.cumsum(logf.reshape(B_, N_HEADS, nc, CHUNK), axis=-1)
    b_last = bcum[..., -1]

    log_w = b_last[..., None] - bcum + igc
    m_loc = jnp.max(log_w, axis=-1)
    w = jnp.exp(log_w - m_loc[..., None])
    kv_loc = jnp.einsum('bhcl,bhcld,bhcle->bhcde', w, kc, vc)
    n_loc = jnp.einsum('bhcl,bhcld->bhcd', w, kc)

    def step(carry, inp):
        C, n, m = carry
        bl, ml, kvl, nl = inp
        m_new = jnp.maximum(bl + m, ml)
        a = jnp.exp(bl + m - m_new)
        s = jnp.exp(ml - m_new)
        C_new = a[..., None, None] * C + s[..., None, None] * kvl
        n_new = a[..., None] * n + s[..., None] * nl
        return (C_new, n_new, m_new), (C, n, m)

    init = (jnp.zeros((B_, N_HEADS, QK_DIM, V_DIM), f32),
            jnp.zeros((B_, N_HEADS, QK_DIM), f32),
            jnp.zeros((B_, N_HEADS), f32))
    xs = (jnp.moveaxis(b_last, 2, 0), jnp.moveaxis(m_loc, 2, 0),
          jnp.moveaxis(kv_loc, 2, 0), jnp.moveaxis(n_loc, 2, 0))
    _, (C_prev, n_prev, m_prev) = lax.scan(step, init, xs)
    C_prev = jnp.moveaxis(C_prev, 0, 2)
    n_prev = jnp.moveaxis(n_prev, 0, 2)
    m_prev = jnp.moveaxis(m_prev, 0, 2)

    causal = jnp.tril(jnp.ones((CHUNK, CHUNK), dtype=bool))
    logD = bcum[..., :, None] - bcum[..., None, :] + igc[..., None, :]
    logD = jnp.where(causal, logD, -jnp.inf)
    log_inter = bcum + m_prev[..., None]
    m_t = jnp.maximum(jnp.max(logD, axis=-1), log_inter)
    Dm = jnp.exp(logD - m_t[..., None])
    scores = jnp.einsum('bhcld,bhcsd->bhcls', qc, kc) * Dm
    inter = jnp.exp(log_inter - m_t)
    num = (jnp.einsum('bhcls,bhcse->bhcle', scores, vc)
           + inter[..., None] * jnp.einsum('bhcld,bhcde->bhcle', qc, C_prev))
    den = jnp.sum(scores, axis=-1) + inter * jnp.einsum('bhcld,bhcd->bhcl', qc, n_prev)
    h = num / jnp.maximum(jnp.abs(den), jnp.exp(-m_t))[..., None]

    h = h.reshape(B_, N_HEADS, S, V_DIM).transpose(0, 2, 1, 3)
    h = h * lax.rsqrt(jnp.mean(h * h, axis=-1, keepdims=True) + EPS)
    h = h * g_hnorm.astype(f32).reshape(N_HEADS, V_DIM)
    h = jax.nn.sigmoid(o.astype(f32)) * h.reshape(B_, S, D_MODEL)
    return h.astype(x.dtype) @ w_out

def short_conv_mixer(x, w_in, w_conv, w_out):
    proj = x @ w_in
    bgate, cgate, xh = jnp.split(proj, 3, axis=-1)
    u = cgate * xh
    conv = lax.conv_general_dilated(
        u, w_conv[:, None, :].astype(u.dtype), window_strides=(1,),
        padding=[(CONV_WIDTH - 1, 0)],
        dimension_numbers=('NWC', 'WIO', 'NWC'),
        feature_group_count=D_MODEL)
    return (bgate * conv) @ w_out

def sqrelu_mlp(x, w_up, w_down):
    h = jax.nn.relu(x @ w_up)
    return (h * h) @ w_down

def first_inputs(seed: int = 0) -> dict:
    key = jax.random.key(seed)
    ks = jax.random.split(key, 12)
    f32 = jnp.float32
    x = jax.random.normal(ks[0], (BATCH, SEQ, D_MODEL), f32)
    norm_g = 1.0 + 0.05 * jax.random.normal(ks[1], (DEPTH, 4, D_MODEL), f32)
    w_in_mlstm = jax.random.normal(ks[2], (N_MLSTM_LAYERS, D_MODEL, MLSTM_IN), f32) * D_MODEL ** -0.5
    i_bias = -3.0 + 0.1 * jax.random.normal(ks[3], (N_MLSTM_LAYERS, N_HEADS), f32)
    f_bias = (jnp.linspace(3.0, 6.0, N_HEADS, dtype=f32)[None, :]
              + 0.1 * jax.random.normal(ks[4], (N_MLSTM_LAYERS, N_HEADS), f32))
    b_gates_mlstm = jnp.concatenate([i_bias, f_bias], axis=-1)
    g_hnorm = 1.0 + 0.05 * jax.random.normal(ks[5], (N_MLSTM_LAYERS, D_MODEL), f32)
    w_out_mlstm = jax.random.normal(ks[6], (N_MLSTM_LAYERS, D_MODEL, D_MODEL), f32) * D_MODEL ** -0.5
    w_in_conv = jax.random.normal(ks[7], (N_CONV_LAYERS, D_MODEL, CONV_IN), f32) * D_MODEL ** -0.5
    w_conv = jax.random.normal(ks[8], (N_CONV_LAYERS, CONV_WIDTH, D_MODEL), f32) * CONV_WIDTH ** -0.5
    w_out_conv = jax.random.normal(ks[9], (N_CONV_LAYERS, D_MODEL, D_MODEL), f32) * D_MODEL ** -0.5
    w_mlp_up = jax.random.normal(ks[10], (DEPTH, D_MODEL, D_FF), f32) * D_MODEL ** -0.5
    w_mlp_down = jax.random.normal(ks[11], (DEPTH, D_FF, D_MODEL), f32) * D_FF ** -0.5
    return {"x": x, "norm_g": norm_g, "w_in_mlstm": w_in_mlstm, "b_gates_mlstm": b_gates_mlstm,
            "g_hnorm": g_hnorm, "w_out_mlstm": w_out_mlstm, "w_in_conv": w_in_conv,
            "w_conv": w_conv, "w_out_conv": w_out_conv, "w_mlp_up": w_mlp_up,
            "w_mlp_down": w_mlp_down}

def first_block(x, norm_g, w_in_mlstm, b_gates_mlstm, g_hnorm, w_out_mlstm, w_in_conv,
              w_conv, w_out_conv, w_mlp_up, w_mlp_down):
    for i in range(DEPTH):
        g = norm_g[i]
        j = i // N_MIXERS
        h = rms_norm(x, g[0])
        if i % N_MIXERS == 0:
            h = mlstm_mixer(h, w_in_mlstm[j], b_gates_mlstm[j], g_hnorm[j], w_out_mlstm[j])
        else:
            h = short_conv_mixer(h, w_in_conv[j], w_conv[j], w_out_conv[j])
        x = x + rms_norm(h, g[1])
        h = sqrelu_mlp(rms_norm(x, g[2]), w_mlp_up[i], w_mlp_down[i])
        x = x + rms_norm(h, g[3])
    return x


DEPTH_2 = 1

N_MEM = 256
D_MIX = D_MODEL
RET_WIDTH = D_MIX // 2
RET_HEADS = 4
RET_HEAD_DIM = RET_WIDTH // RET_HEADS
POOL_WIDTH = D_MIX - RET_WIDTH
POOL_WINDOWS = (2, 4, 8, 16)
POOL_GROUP = POOL_WIDTH // len(POOL_WINDOWS)
IN_COLS = 4 * RET_WIDTH + POOL_WIDTH
ROPE_BASE = 10000.0
XA_HEADS = 4
XA_HEAD_DIM = D_MODEL // XA_HEADS
D_FF_2 = ((8 * D_MODEL // 3 + 255) // 256) * 256


def rmsnorm(x, g):
    x32 = x.astype(jnp.float32)
    y = x32 * lax.rsqrt(jnp.mean(x32 * x32, axis=-1, keepdims=True) + EPS)
    return (y * g.astype(jnp.float32)).astype(x.dtype)

def rope(t, positions):
    dh = t.shape[-1]
    inv_freq = jnp.exp(-math.log(ROPE_BASE) * jnp.arange(0, dh, 2, dtype=jnp.float32) / dh)
    ang = positions.astype(jnp.float32)[..., None] * inv_freq
    cos = jnp.cos(ang)[:, :, None, :].astype(t.dtype)
    sin = jnp.sin(ang)[:, :, None, :].astype(t.dtype)
    t1, t2 = jnp.split(t, 2, axis=-1)
    return jnp.concatenate([t1 * cos - t2 * sin, t2 * cos + t1 * sin], axis=-1)

def retention(q, k, v, positions):
    B, S, _ = q.shape
    H, Dh = RET_HEADS, RET_HEAD_DIM
    dt = q.dtype
    N = S // CHUNK
    q = rope(q.reshape(B, S, H, Dh), positions)
    k = rope(k.reshape(B, S, H, Dh), positions) * (Dh ** -0.5)
    v = v.reshape(B, S, H, Dh)

    def to_chunks(t):
        return t.reshape(B, N, CHUNK, H, Dh).transpose(0, 3, 1, 2, 4)

    qc, kc, vc = to_chunks(q), to_chunks(k), to_chunks(v)
    lg = jnp.log1p(-jnp.exp2(-5.0 - jnp.arange(H, dtype=jnp.float32)))
    idx = jnp.arange(CHUNK, dtype=jnp.float32)
    diff = idx[:, None] - idx[None, :]
    dmat = jnp.where(diff >= 0, jnp.exp(lg[:, None, None] * jnp.maximum(diff, 0.0)), 0.0).astype(dt)
    zeta = jnp.exp(lg[:, None] * (CHUNK - 1 - idx)).astype(dt)
    xi = jnp.exp(lg[:, None] * (idx + 1.0)).astype(dt)
    chunk_decay = jnp.exp(lg * CHUNK).astype(dt)

    scores = jnp.einsum('bhnid,bhnjd->bhnij', qc, kc) * dmat[:, None]
    intra = jnp.einsum('bhnij,bhnjv->bhniv', scores, vc)
    kv = jnp.einsum('bhnjd,bhnjv->nbhdv', kc * zeta[:, None, :, None], vc)

    def step(state, kv_n):
        return state * chunk_decay[None, :, None, None] + kv_n, state

    _, states_before = lax.scan(step, jnp.zeros((B, H, Dh, Dh), dt), kv)
    cross = jnp.einsum('bhnid,nbhdv->bhniv', qc, states_before) * xi[:, None, :, None]
    return (intra + cross).transpose(0, 2, 3, 1, 4).reshape(B, S, H, Dh)

def head_rmsnorm(y, g):
    B, S, H, Dh = y.shape
    y32 = y.astype(jnp.float32)
    y32 = y32 * lax.rsqrt(jnp.mean(y32 * y32, axis=-1, keepdims=True) + EPS)
    return (y32.reshape(B, S, H * Dh) * g.astype(jnp.float32)).astype(y.dtype)

def pool_mixer(u, w, scale):
    B, S, _ = u.shape
    u32 = u.astype(jnp.float32)
    cs = jnp.cumsum(u32, axis=1)
    t1 = jnp.arange(1, S + 1, dtype=jnp.int32)
    groups = []
    for gi, wlen in enumerate(POOL_WINDOWS):
        c = cs[:, :, gi * POOL_GROUP:(gi + 1) * POOL_GROUP]
        lower = jnp.concatenate([jnp.zeros((B, wlen, POOL_GROUP), jnp.float32), c[:, :S - wlen]], axis=1)
        count = jnp.minimum(t1, wlen).astype(jnp.float32)[None, :, None]
        mean = (c - lower) / count
        groups.append(mean - u32[:, :, gi * POOL_GROUP:(gi + 1) * POOL_GROUP])
    pooled = jnp.stack(groups, axis=2).astype(u.dtype)
    out = jnp.einsum('bsgc,gcd->bsgd', pooled, w).reshape(B, S, POOL_WIDTH)
    return out * scale

def cross_attn(h, mem_n, wq, wkv, wo):
    B, S, _ = h.shape
    q = (h @ wq).reshape(B, S, XA_HEADS, XA_HEAD_DIM)
    k, v = jnp.split(mem_n @ wkv, 2, axis=-1)
    k = k.reshape(B, N_MEM, XA_HEADS, XA_HEAD_DIM)
    v = v.reshape(B, N_MEM, XA_HEADS, XA_HEAD_DIM)
    s = jnp.einsum('bshd,bmhd->bhsm', q, k).astype(jnp.float32) * (XA_HEAD_DIM ** -0.5)
    p = jax.nn.softmax(s, axis=-1).astype(v.dtype)
    o = jnp.einsum('bhsm,bmhd->bshd', p, v).reshape(B, S, D_MODEL)
    return o @ wo

def conv_glu_ffn(h, w_up, conv_w, conv_b, w_down):
    a = h @ w_up
    S = a.shape[1]
    a1 = jnp.pad(a, ((0, 0), (1, 0), (0, 0)))[:, :S]
    a2 = jnp.pad(a, ((0, 0), (2, 0), (0, 0)))[:, :S]
    c = conv_w[0] * a2 + conv_w[1] * a1 + conv_w[2] * a + conv_b
    gate, val = jnp.split(c, 2, axis=-1)
    return (jax.nn.silu(gate) * val) @ w_down

def second_inputs(seed: int = 0) -> dict:
    key = jax.random.key(seed)
    ks = jax.random.split(key, 24)

    def nrm(k, shape, scale):
        return jax.random.normal(k, shape, jnp.float32) * scale

    L = DEPTH_2
    x = nrm(ks[0], (BATCH, SEQ, D_MODEL), 1.0)
    mem = nrm(ks[1], (BATCH, N_MEM, D_MODEL), 1.0)
    offs = jax.random.randint(ks[2], (BATCH, 1), 0, 1024, dtype=jnp.int32)
    positions = (offs + jnp.arange(SEQ, dtype=jnp.int32)[None, :]).astype(jnp.int32)
    return {
        "x": x,
        "mem": mem,
        "positions": positions,
        "mix_norm_g": 1.0 + nrm(ks[3], (L, D_MODEL), 0.02),
        "w_in": nrm(ks[4], (L, D_MODEL, IN_COLS), D_MODEL ** -0.5),
        "ret_gn_g": 1.0 + nrm(ks[5], (L, RET_WIDTH), 0.02),
        "pool_w": nrm(ks[6], (L, len(POOL_WINDOWS), POOL_GROUP, POOL_GROUP), POOL_GROUP ** -0.5),
        "pool_scale": 0.5 + nrm(ks[7], (L, POOL_WIDTH), 0.1),
        "w_out": nrm(ks[8], (L, D_MIX, D_MODEL), (2.0 * D_MIX) ** -0.5),
        "xa_norm_g": 1.0 + nrm(ks[9], (L, D_MODEL), 0.02),
        "mem_norm_g": 1.0 + nrm(ks[10], (D_MODEL,), 0.02),
        "xa_wq": nrm(ks[11], (L, D_MODEL, D_MODEL), D_MODEL ** -0.5),
        "xa_wkv": nrm(ks[12], (L, D_MODEL, 2 * D_MODEL), D_MODEL ** -0.5),
        "xa_wo": nrm(ks[13], (L, D_MODEL, D_MODEL), (2.0 * D_MODEL) ** -0.5),
        "ffn_norm_g": 1.0 + nrm(ks[14], (L, D_MODEL), 0.02),
        "ffn_w_up": nrm(ks[15], (L, D_MODEL, 2 * D_FF_2), D_MODEL ** -0.5),
        "ffn_conv_w": nrm(ks[16], (L, CONV_WIDTH, 2 * D_FF_2), CONV_WIDTH ** -0.5),
        "ffn_conv_b": nrm(ks[17], (L, 2 * D_FF_2), 0.01),
        "ffn_w_down": nrm(ks[18], (L, D_FF_2, D_MODEL), (2.0 * D_FF_2) ** -0.5),
        "final_norm_g": 1.0 + nrm(ks[19], (D_MODEL,), 0.02),
    }

def second_block(x, mem, positions, mix_norm_g, w_in, ret_gn_g, pool_w, pool_scale, w_out,
              xa_norm_g, mem_norm_g, xa_wq, xa_wkv, xa_wo, ffn_norm_g, ffn_w_up,
              ffn_conv_w, ffn_conv_b, ffn_w_down, final_norm_g):
    mem_n = rmsnorm(mem, mem_norm_g)
    R = RET_WIDTH
    for l in range(DEPTH_2):
        h = rmsnorm(x, mix_norm_g[l])
        proj = h @ w_in[l]
        q, k, v, g, u = jnp.split(proj, [R, 2 * R, 3 * R, 4 * R], axis=-1)
        y_ret = jax.nn.silu(g) * head_rmsnorm(retention(q, k, v, positions), ret_gn_g[l])
        y_pool = pool_mixer(u, pool_w[l], pool_scale[l])
        x = x + jnp.concatenate([y_ret, y_pool], axis=-1) @ w_out[l]
        x = x + cross_attn(rmsnorm(x, xa_norm_g[l]), mem_n, xa_wq[l], xa_wkv[l], xa_wo[l])
        x = x + conv_glu_ffn(rmsnorm(x, ffn_norm_g[l]), ffn_w_up[l], ffn_conv_w[l],
                             ffn_conv_b[l], ffn_w_down[l])
    return rmsnorm(x, final_norm_g)


def setup_inputs(seed=0):
    out = dict(first_inputs(seed))
    for name, value in second_inputs(seed + 1).items():
        if name != "x":
            out[name + "_2"] = value
    return out


def reference(
    x, norm_g, w_in_mlstm, b_gates_mlstm, g_hnorm, w_out_mlstm, w_in_conv, w_conv, w_out_conv,
    w_mlp_up, w_mlp_down, mem_2, positions_2, mix_norm_g_2, w_in_2, ret_gn_g_2, pool_w_2,
    pool_scale_2, w_out_2, xa_norm_g_2, mem_norm_g_2, xa_wq_2, xa_wkv_2, xa_wo_2, ffn_norm_g_2,
    ffn_w_up_2, ffn_conv_w_2, ffn_conv_b_2, ffn_w_down_2, final_norm_g_2,
):
    x = first_block(
        x, norm_g, w_in_mlstm, b_gates_mlstm, g_hnorm, w_out_mlstm, w_in_conv, w_conv,
        w_out_conv, w_mlp_up, w_mlp_down,
    )
    return second_block(
        x, mem_2, positions_2, mix_norm_g_2, w_in_2, ret_gn_g_2, pool_w_2, pool_scale_2,
        w_out_2, xa_norm_g_2, mem_norm_g_2, xa_wq_2, xa_wkv_2, xa_wo_2, ffn_norm_g_2,
        ffn_w_up_2, ffn_conv_w_2, ffn_conv_b_2, ffn_w_down_2, final_norm_g_2,
    )


_drawn_inputs = setup_inputs


def setup_inputs(seed=0):
    import zlib

    import numpy as np

    out = dict(_drawn_inputs(seed))
    spreads = {}
    factors = {'mix_norm_g_2': 8.0,
     'ret_gn_g_2': 8.0,
     'pool_scale_2': 3.168,
     'xa_norm_g_2': 8.0,
     'mem_norm_g_2': 8.0,
     'ffn_norm_g_2': 8.0,
     'ffn_conv_b_2': 39.329}
    for name, (base, spread) in spreads.items():
        noise = np.random.default_rng([zlib.crc32(name.encode()), seed]).standard_normal(out[name].shape)
        drawn = base * np.exp(spread * noise) if base else spread * noise
        out[name] = __import__('jax').numpy.asarray(drawn.astype(out[name].dtype))
    for name, factor in factors.items():
        out[name] = (out[name] * factor).astype(out[name].dtype)
    return out
```

```python
import math
from contextlib import ExitStack

import numpy as np

import concourse.bass as bass
from concourse import mybir

P = 128
T = 256
TT = T // P
D = 1024
C = D // P
F1 = 4 * D
F2 = ((8 * D // 3 + 255) // 256) * 256
NH = 4
QK = D // (2 * NH)
VD = D // NH
RW = D // 2
RH = RW // NH
XH = D // NH
WINDOWS = (2, 4, 8, 16)
EPS = 1e-6
CAP = 15.0
ROPE_BASE = 10000.0
BLOCKED = -1.0e30

SLAB = 16 * P
HALF = SLAB // 2
RAW = 4
HL = 2

K_FILL, V_FILL = "K_FILL", "V_FILL"
PHASES = [
    ("qk", 4, 4, "V"), ("v", 4, 4, "A"), ("o", 4, 4, "V"), ("f0", 1, 1, "V"),
    ("out0", 4, 4, "A"), ("f1", 1, 1, "V"), ("up0", 16, 16, "V"), ("down0", 16, 4, "A"), ("f2", 1, 1, "V"),
    ("cin", 12, 12, "AVV"), ("f3", 1, 1, "V"), ("out1", 4, 4, "A"), ("f4", 1, 1, "A"),
    ("up1", 16, 16, "V"), ("down1", 16, 4, "A"), ("f5", 1, 1, "A"),
    ("rq", 4, 4, "V"), ("rv", 2, 2, "A"), ("rug", 4, 4, "V"), ("f6", 1, 1, "A"), ("out2", 4, 4, "V"),
    ("wq", 4, 4, "V"), ("f7", 1, 1, "A"), ("wo", 4, 4, "V"),
    ("fup", 2 * F2 // 256, 2 * F2 // 256, "V"), ("fdown", F2 // P // 2, 4, "V"),
]
SLAB0, GROUP0, DRAIN = {}, {}, []
_s = _g = 0
_count = {"A": 0, "V": 0}
for _name, _ns, _ng, _eng in PHASES:
    SLAB0[_name], GROUP0[_name] = _s, _g
    for _i in range(_ng):
        _e = _eng[_i % len(_eng)]
        _count[_e] += 1
        DRAIN.append((_e, _count[_e]))
    _s, _g = _s + _ns, _g + _ng
SLABS = _s

PCOL, _c = {}, 0
for _name, _n in [("g00", C), ("g01", C), ("g02", C), ("g03", C), ("g10", C), ("g11", C), ("g12", C), ("g13", C),
                  ("ghn", C), ("wconv", 3 * C), ("gmix", C), ("gret", NH), ("pscale", NH), ("gxa", C), ("gmem", C),
                  ("gffn", C), ("fw", 3 * 2 * F2 // P), ("fb", 2 * F2 // P), ("gfin", C), ("bgates", 2 * NH)]:
    PCOL[_name] = _c
    _c += _n
NPAR = _c
FT = 2 * F2 // P
FC = F2 // P

NORMS = ["pre", "pre", "post", "pre", "post", "pre", "post", "pre", "post", "pre", "pre", "pre", "last"]


def build(nc, xT, memT, pos, weights, wgate, params, poolw, tri, mask, select, decay, freq, recount, out):
    f32, f32r, i32 = mybir.dt.float32, mybir.dt.float32r, mybir.dt.int32
    ALU, ACT, AX = mybir.AluOpType, mybir.ActivationFunctionType, mybir.AxisListType

    ctx = ExitStack()
    with ctx:
        place = [nc.sbuf_base + (-nc.sbuf_base) % 64]

        def sb(name, shape, dt, at=None):
            size = int(np.prod(shape[1:])) * 4
            if at is None:
                off = place[0]
                place[0] += (size + 31) // 32 * 32
            else:
                off = at[0]
                at[0] += (size + 31) // 32 * 32
            return nc.alloc_sbuf_tensor_at(name, list(shape), dt, offset=off)

        def sem(name):
            return ctx.enter_context(nc.semaphore(name))

        raw = [sb(f"raw{i}", [P, SLAB], f32) for i in range(RAW)]
        wH = [sb(f"wH{i}", [P, SLAB], f32r) for i in range(HL)]
        wL = [sb(f"wL{i}", [P, SLAB], f32r) for i in range(HL)]
        x = sb("x", [P, C, T], f32)
        xnH = sb("xnH", [P, C, T], f32r)
        xnL = sb("xnL", [P, C, T], f32r)
        memH = sb("memH", [P, C, T], f32r)
        memL = sb("memL", [P, C, T], f32r)
        memk = sb("memk", [P, C, T], f32)
        memv = sb("memv", [P, TT, D], f32)
        ident = sb("ident", [P, P], f32)
        ones = sb("ones", [P, P], f32)
        par = sb("par", [P, NPAR], f32)
        Rs = sb("Rs", [P, T], f32)
        Rm = sb("Rm", [P, T], f32)
        diag = sb("diag", [P, TT, P], f32)
        ms = sb("ms", [P, TT], f32)
        minus_half = sb("minus_half", [P, 2 * NH], f32)
        rtok = sb("rtok", [P, TT], f32)
        rmem = sb("rmem", [P, TT], f32)
        scratch = place[0]
        at = [scratch]
        y = sb("y", [P, C, T], f32, at)
        squares = sb("squares", [P, 4, 2, T], f32, at)
        sq = [squares[:, i, :, :] for i in range(4)]
        end = at[0]
        at = [scratch]
        hrelu = [sb(f"hrelu{i}", [P, 2, T], f32, at) for i in range(2)]
        hsq = [sb(f"hsq{i}", [P, 2, T], f32, at) for i in range(2)]
        at = [scratch]
        mem = sb("mem", [P, C, T], f32, at)
        at = [scratch]
        apad = [sb(f"apad{i}", [P, 2, T + 2], f32, at) for i in range(2)]
        cgate = sb("cgate", [P, 2, T], f32, at)
        cval = sb("cval", [P, 2, T], f32, at)
        assert at[0] <= scratch + C * T * 4 + 64
        place[0] = end
        region = place[0]
        at = [region]
        hH = sb("hH", [P, F1 // P, T], f32r, at)
        hL = sb("hL", [P, F1 // P, T], f32r, at)
        place[0] = at[0]

        at = [region]
        mixH = sb("mixH", [P, C, T], f32r, at)
        mixL = sb("mixL", [P, C, T], f32r, at)
        mixer = at[0]
        used = [at[0]]
        qT = sb("qT", [P, NH, T], f32, at)
        kT = sb("kT", [P, NH, T], f32, at)
        vx = sb("vx", [P, TT, NH, VD + 1], f32, at)
        sigo = sb("sigo", [P, C, T], f32, at)
        trit = sb("trit", [P, P], f32, at)
        maskt = sb("maskt", [P, T], f32, at)
        selt = sb("selt", [NH, NH, P], f32, at)
        used2 = [at[0]]
        dargs = sb("dargs", [P, T + P], f32, at)
        dexp = sb("dexp", [P, T + P], f32, at)
        prob = [sb(f"prob{h}", [P, T + P], f32, at) for h in range(NH)]
        num = [sb(f"num{i}", [P, TT, VD + 1], f32, used) for i in range(2)]
        hn = [sb(f"hn{i}", [P, TT, VD], f32, w) for i, w in enumerate((used, at))]
        junk = sb("junk", [P, VD], f32, at)
        mixf = sb("mixf", [P, 2, T], f32, used2)
        wg = sb("wg", [P, C, 2 * NH], f32, at)
        wgs = sb("wgs", [P, C, 2 * NH], f32, at)
        gz = sb("gz", [P, TT, 2 * NH], f32, at)
        gt = sb("gt", [P, TT, 2 * NH], f32, at)
        gcap = sb("gcap", [P, TT, 2 * NH], f32, at)
        fexp = sb("fexp", [P, TT, NH], f32, at)
        softp = sb("softp", [P, TT, NH], f32, at)
        nb = sb("nb", [P, TT, NH], f32, at)
        av = sb("av", [P, TT, NH], f32, at)
        mrow = [sb(f"mrow{i}", [NH, P + T], f32, at) for i in range(2)]
        mdiff = sb("mdiff", [P, TT, NH], f32, at)
        em = sb("em", [P, TT, NH], f32, at)
        ssq = sb("ssq", [P, NH, TT], f32, at)
        den = sb("den", [P, NH, TT], f32, at)
        rec = sb("rec", [P, NH, TT], f32, at)
        rec2 = sb("rec2", [P, NH, TT], f32, at)
        hms = sb("hms", [P, NH, TT], f32, at)
        hr = sb("hr", [P, NH, TT], f32, at)
        hc = sb("hc", [P, NH, TT], f32, at)
        assert at[0] <= place[0], at
        at = [mixer]
        csb = sb("csb", [P, 2, T], f32, at)
        cx = sb("cx", [P, 2, T], f32, at)
        upad = sb("upad", [P, 2, T + 2], f32, at)
        conv = sb("conv", [P, 2, T], f32, at)
        bsb = sb("bsb", [P, 2, T], f32, at)
        cout = sb("cout", [P, 2, T], f32, at)
        R2 = sb("R2", [P, T], f32, at)
        at = [mixer]
        rq = sb("rq", [P, NH, T], f32, at)
        rk = sb("rk", [P, NH, T], f32, at)
        rv = sb("rv", [P, TT, RW], f32, at)
        rsg = sb("rsg", [P, NH, T], f32, at)
        rop = sb("rop", [P, 2, T], f32, at)
        rot = sb("rot", [P, 2, T], f32, at)
        ropc = sb("ropc", [P, 2, T], f32, at)
        rops = sb("rops", [P, 2, T], f32, at)
        cost = sb("cost", [P, T], f32, at)
        sint = sb("sint", [P, T], f32, at)
        freqt = sb("freqt", [P, 1], f32, at)
        halfpi = sb("halfpi", [P, 1], f32, at)
        decayt = sb("decayt", [P, NH, T], f32, at)
        angles = [at[0]]
        posi = sb("posi", [P, T], i32, angles)
        ang = sb("ang", [P, T], f32, angles)
        turn = sb("turn", [P, T], f32, angles)
        rs = [sb(f"rs{i}", [P, T + P], f32, at) for i in range(2)]
        ro = sb("ro", [P, NH, T], f32, at)
        rosq = sb("rosq", [P, NH, T], f32, at)
        at2 = [at[0]]
        rms8 = sb("rms8", [P, NH, TT], f32, at2)
        rr8 = sb("rr8", [P, NH, TT], f32, at2)
        rdiag = sb("rdiag", [P, 2, TT, P], f32, at2)
        poolwt = sb("poolwt", [P, NH, P], f32, at2)
        recountt = sb("recountt", [P, NH, 16], f32, at2)
        PADW = 16
        upl = sb("upl", [P, 2, PADW + T], f32, at2)
        sl = [sb(f"sl{i}", [P, PADW + T], f32, at2) for i in range(2)]
        place[0] = max(place[0], at2[0])
        pooled, yret = ropc, rops
        at = [mixer]
        xq = [sb(f"xq{i}", [P, 2, T], f32, at) for i in range(2)]
        xp = [sb(f"xp{i}", [P, TT, T], f32, at) for i in range(2)]
        xpn = [sb(f"xpn{i}", [P, TT, T], f32, at) for i in range(2)]
        xpT = [sb(f"xpT{i}", [P, TT, T], f32, at) for i in range(2)]
        xmax = sb("xmax", [P, NH, TT], f32, at)
        xneg = sb("xneg", [P, NH, TT], f32, at)
        xsum = sb("xsum", [P, NH, TT], f32, at)
        xrec = sb("xrec", [P, NH, TT], f32, at)
        outT = xq
        assert place[0] <= nc.sbuf_usable_end, (place, nc.sbuf_usable_end)

        po = [ctx.enter_context(nc.psum_tensor(f"po{i}", [P, 2, 512], f32)) for i in range(2)]
        pn = ctx.enter_context(nc.psum_tensor("pn", [P, 512], f32))
        pa = ctx.enter_context(nc.psum_tensor("pa", [P, 512], f32))
        pb = ctx.enter_context(nc.psum_tensor("pb", [P, 512], f32))
        pc = ctx.enter_context(nc.psum_tensor("pc", [P, 512], f32))

        s_raw = [sem(f"raw_loaded{i}") for i in range(RAW)]
        s_hi, s_lo = sem("weights_hi"), sem("weights_lo")
        s_slab = sem("slab_done")
        s_group = sem("glu_group_done")
        s_drain = {"A": sem("drained_act"), "V": sem("drained_dve")}
        s_par, s_cst, s_mem = sem("params_loaded"), sem("consts_loaded"), sem("mem_loaded")
        s_x = [sem(f"x_loaded{i}") for i in range(4)]
        s_set = sem("constants_set")
        s_xnH, s_xn = sem("xn_hi"), sem("xn_ready")
        s_sq, s_sqa = sem("squares"), sem("squares_added")
        s_sum, s_ms, s_r, s_diag, s_R = sem("sumsq"), sem("mean_sq"), sem("r_ready"), sem("diag_ready"), sem("R_done")
        s_Rs = sem("R_kept")
        s_t, s_xadd = sem("y_scaled"), sem("x_added")
        s_mmH, s_mm = sem("mem_hi"), sem("mem_ready")
        s_dch, s_ach, s_pch = sem("dve_chain"), sem("act_chain"), sem("pool_chain")
        s_mixH, s_mix = sem("mix_hi"), sem("mix_ready")
        s_relu, s_hs, s_hidH, s_hid = sem("relu_ready"), sem("h_squared"), sem("hidden_hi"), sem("hidden_ready")
        s_gates, s_gz, s_gt, s_gcap, s_fe, s_sp = [sem("g_" + n) for n in ("mm", "z", "tanh", "cap", "fexp", "softplus")]
        s_wgs, s_cum, s_av, s_avT, s_mrow, s_mT, s_md, s_em = [
            sem("m_" + n) for n in ("wgs", "cum", "av", "avT", "mrow", "mT", "md", "em")]
        s_osig = sem("o_sigmoid")
        s_S, s_darg, s_dexp, s_P, s_num, s_numk = [sem("a_" + n) for n in ("S", "darg", "dexp", "P", "num", "numk")]
        s_hms, s_hr, s_hn, s_hT, s_mixf = [sem("h_" + n) for n in ("ms", "r", "n", "T", "mixf")]
        s_c, s_u, s_cv, s_cvd, s_cf = [sem("c_" + n) for n in ("gate", "u", "tap", "conv", "out")]
        s_pos, s_rc = sem("r_pos"), sem("r_consts")
        s_trig, s_trigd = sem("r_angle"), sem("r_trig")
        s_rop, s_rot, s_rqk, s_rv = [sem("r_" + n) for n in ("rop", "rot", "qk", "v")]
        s_rS, s_rs, s_rO, s_ro = [sem("r_" + n) for n in ("S", "s", "O", "o")]
        s_rg, s_rsg, s_rsum, s_rms, s_rr, s_rdiag, s_rR, s_ry = [
            sem("r_" + n) for n in ("gate", "silu", "sum", "ms", "r", "diag", "R", "y")]
        s_ul, s_sl, s_pool, s_pw, s_pf = [sem("p_" + n) for n in ("u", "sums", "pooled", "mm", "out")]
        s_rRused = sem("r_Rused")
        s_xq, s_xs, s_xneg, s_xe, s_xpn, s_xT, s_xpT, s_xo = [
            sem("x_" + n) for n in ("q", "s", "neg", "exp", "norm", "T", "pT", "o")]
        s_fa, s_fc, s_fcd, s_fs, s_fh, s_fH, s_f = [
            sem("f_" + n) for n in ("a", "tap", "conv", "silu", "h", "hi", "ready")]
        s_outv, s_out = sem("out_ready"), sem("stored")

        def col(name, i=0, n=1):
            return par[:, PCOL[name] + i:PCOL[name] + i + n]

        def over_pair(ap):
            return ap.rearrange("p (a t) -> p a t", a=1).to_broadcast([P, 2, T])

        def slot(g):
            return po[g % 2]

        def kept_before(norm):
            pre = sum(k == "pre" for k in NORMS[:norm])
            return pre, norm - pre

        block = ctx.enter_context(nc.Block())

        @block.sync
        def _(sp):
            sp.dma_start(par[:, :], params).then_inc(s_par, 16)
            for p in range(4):
                sp.dma_start(x[:, 2 * p:2 * p + 2, :], xT[:, 2 * p:2 * p + 2, :]).then_inc(s_x[p], 16)
            for s in range(RAW):
                sp.dma_start(raw[s][:, :], weights[s, :, :]).then_inc(s_raw[s], 16)
                if s == 0:
                    for k, (dst, src) in enumerate([(ident[:, :], tri[1, :, :]), (wg[:, :, :], wgate), (trit[:, :], tri[0, :, :]),
                                     (maskt[:, :], mask), (selt[:, :, :], select)]):
                        sp.dma_start(dst, src).then_inc(s_cst, 16)
                        if k == 0:
                            sp.wait_ge(s_cst, 16)
                    sp.wait_ge(s_cst, 80)
                    sp.dma_start(mem[:, :, :], memT).then_inc(s_mem, 16)

            def load(s, slot_):
                sp.wait_ge(s_lo, s * 2 - 6)
                sp.dma_start(raw[slot_][:, :], weights[s, :, :]).then_inc(s_raw[slot_], 16)

            stop = SLAB0["rq"] // RAW + 1
            with sp.Fori(1, stop) as i:
                for j in range(RAW):
                    load(i * RAW + j, j)
            sp.wait_ge(s_slab, SLAB0["f5"])
            for k, (dst, src) in enumerate([(posi[:, :], pos.partition_broadcast(P)), (freqt[:, :], freq)]):
                sp.dma_start(dst, src).then_inc(s_pos, 16)
            for dst, src in [(decayt[:, :, :], decay), (poolwt[:, :, :], poolw), (recountt[:, :, :], recount)]:
                sp.dma_start(dst, src).then_inc(s_rc, 16)
            with sp.Fori(stop, SLABS // RAW) as i:
                for j in range(RAW):
                    load(i * RAW + j, j)
            for s in range(SLABS // RAW * RAW, SLABS):
                load(s, s % RAW)
            for p in range(4):
                sp.wait_ge(s_outv, p + 1)
                sp.dma_start(out[:, 2 * p:2 * p + 2, :], y[:, 2 * p:2 * p + 2, :]).then_inc(s_out, 16)
            sp.wait_ge(s_out, 64)

        @block.tensor
        def _(pe):
            def weights_ready(s, half):
                pe.wait_ge(s_lo, s * 2 + half + 1)

            def slot_free(g):
                if g >= 2:
                    e, n = DRAIN[g - 2]
                    pe.wait_ge(s_drain[e], n)

            def products(psum, n, w, k, aH, aL, ac, start, stop):
                wc = slice(k * 256 + n * P, k * 256 + (n + 1) * P)
                pe.matmul(psum[:, n, 0:T], wH[w][:, wc], aH[:, ac, :], start=start, stop=False)
                pe.matmul(psum[:, n, 0:T], wH[w][:, wc], aL[:, ac, :], start=False, stop=False)
                return pe.matmul(psum[:, n, 0:T], wL[w][:, wc], aH[:, ac, :], start=False, stop=stop)

            def slab(s, w, psum, aH, aL, c0=0, first=True, last=True, ready=None, between={}):
                for k in range(8):
                    if k % 4 == 0:
                        weights_ready(s, k // 4)
                    if ready and k % 2 == 0:
                        pe.wait_ge(ready[0], ready[1] + k // 2 + 1)
                    for n in range(2):
                        mm = products(psum, n, w, k, aH, aL, c0 + k, first and k == 0, last and k == 7)
                    if k in between:
                        between[k]()
                mm.then_inc(s_slab, 1)

            def slab_by_token(s, w, psum, aH, aL, between={}):
                for k in range(8):
                    if k % 4 == 0:
                        weights_ready(s, k // 4)
                    wc = slice(k * 256, k * 256 + 256)
                    for t in range(TT):
                        tc = slice(t * P, t * P + P)
                        pe.matmul(psum[:, t, 0:256], aH[:, k, tc], wH[w][:, wc], start=k == 0, stop=False)
                        pe.matmul(psum[:, t, 0:256], aL[:, k, tc], wH[w][:, wc], start=False, stop=False)
                        mm = pe.matmul(psum[:, t, 0:256], aH[:, k, tc], wL[w][:, wc], start=False, stop=k == 7)
                    if k in between:
                        between[k]()
                mm.then_inc(s_slab, 1)

            def phase_slab(name, i, aH, aL, by_token=False, ready=None, between={}):
                s, g = SLAB0[name] + i, GROUP0[name] + i
                slot_free(g)
                if by_token:
                    slab_by_token(s, s % HL, slot(g), aH, aL, between)
                else:
                    slab(s, s % HL, slot(g), aH, aL, ready=ready, between=between)

            def fill(n, between={}):
                if n == 0:
                    pe.wait_ge(s_mm, 4)
                phase_slab(f"f{n}", 0, memH, memL, by_token=n >= 4, between=between)

            def norm_sums(n):
                if n:
                    pre, other = kept_before(n)
                    if NORMS[n - 1] == "pre":
                        pe.wait_ge(s_Rs, pre)
                    else:
                        pe.wait_ge(s_t, 4 * other)
                pe.wait_ge(s_sqa, 2 * n + 2)
                pe.wait_ge(s_sq, 4 * n + 4)
                for t in range(TT):
                    tc = slice(t * P, t * P + P)
                    parts = [sq[0][:, 0, tc], sq[0][:, 1, tc], sq[3][:, 0, tc], sq[3][:, 1, tc]]
                    for k, part in enumerate(parts):
                        mm = pe.matmul(pn[:, t:t + 1], part, ones[:, 0:1], start=k == 0, stop=k == 3)
                mm.then_inc(s_sum, 1)

            def norm_spread(n):
                pe.wait_ge(s_diag, n + 1)
                for t in range(TT):
                    mm = pe.matmul(pn[:, 128 + t * P:128 + (t + 1) * P], ones[:, :], diag[:, t, :], start=True, stop=True)
                mm.then_inc(s_R, 1)

            def norm(n):
                norm_sums(n)
                norm_spread(n)

            def scores(h):
                if h:
                    pe.wait_ge(s_P, h)
                    pe.wait_ge(s_darg, h)
                pe.matmul(pa[:, 0:T], kT[:, h, 0:P], qT[:, h, :], start=True, stop=True)
                pe.matmul(pa[:, T:T + P], kT[:, h, P:T], qT[:, h, P:T], start=True, stop=True)
                pe.matmul(pb[:, 0:T], selt[:, h, :], mrow[0][:, P:P + T], start=True, stop=True).then_inc(s_S, 1)

            def numerator(h):
                pe.wait_ge(s_P, h + 1)
                pe.wait_ge(s_drain["A"], h + 1)
                if h == 0:
                    pe.wait_ge(s_darg, NH)
                else:
                    pe.wait_ge(s_numk, h)
                pe.matmul(pc[:, 0:VD + 1], prob[h][:, 0:P], vx[:, 0, h, :], start=True, stop=True)
                pe.matmul(pb[:, 0:VD + 1], prob[h][:, P:T], vx[:, 0, h, :], start=True, stop=False)
                pe.matmul(pb[:, 0:VD + 1], prob[h][:, T:T + P], vx[:, 1, h, :], start=False, stop=True)\
                    .then_inc(s_num, 1)

            def turn_head(h):
                pe.wait_ge(s_hn, h + 1)
                if h:
                    pe.wait_ge(s_mixf, h)
                for e in range(2):
                    for t in range(TT):
                        mm = pe.transpose(pn[:, e * T + t * P:e * T + t * P + P],
                                          hn[h % 2][:, t, e * P:(e + 1) * P], ident[:, :])
                mm.then_inc(s_hT, 1)

            phase_slab("qk", 0, xnH, xnL, ready=(s_xn, 0))
            pe.wait_ge(s_set, 1)
            norm(0)
            phase_slab("qk", 1, xnH, xnL)
            pe.wait_ge(s_wgs, 1)
            for t in range(TT):
                for k in range(C):
                    mm = pe.matmul(pa[:, t * 8:t * 8 + 8], x[:, k, t * P:(t + 1) * P], wgs[:, k, :], start=k == 0, stop=k == C - 1)
            mm.then_inc(s_gates, 1)
            phase_slab("qk", 2, xnH, xnL)
            pe.wait_ge(s_sp, 1)
            pe.wait_ge(s_gz, 1)
            pe.matmul(pa[:, 0:NH], trit[:, :], softp[:, 0, :], start=True, stop=True)
            pe.matmul(pa[:, NH:2 * NH], trit[:, :], softp[:, 1, :], start=True, stop=False)
            pe.matmul(pa[:, NH:2 * NH], ones[:, :], softp[:, 0, :], start=False, stop=True).then_inc(s_cum, 1)
            phase_slab("qk", 3, xnH, xnL)
            pe.wait_ge(s_av, 1)
            for t in range(TT):
                mm = pe.transpose(pb[0:NH, t * P:(t + 1) * P], av[:, t, :], ident[:, :])
            mm.then_inc(s_avT, 1)
            phase_slab("v", 0, xnH, xnL, by_token=True)
            pe.wait_ge(s_mrow, 1)
            for t in range(TT):
                mm = pe.transpose(pc[:, t * NH:(t + 1) * NH], mrow[0][:, P + t * P:P + (t + 1) * P], ident[0:NH, 0:NH])
            mm.then_inc(s_mT, 1)
            phase_slab("v", 1, xnH, xnL, by_token=True)
            pe.wait_ge(s_drain["V"], 4)
            scores(0)
            phase_slab("v", 2, xnH, xnL, by_token=True)
            scores(1)
            phase_slab("v", 3, xnH, xnL, by_token=True)
            scores(2)
            phase_slab("o", 0, xnH, xnL)
            scores(3)
            phase_slab("o", 1, xnH, xnL)
            norm(1)
            pe.wait_ge(s_md, 1)
            numerator(0)
            phase_slab("o", 2, xnH, xnL)
            numerator(1)
            pe.wait_ge(s_Rs, 2)
            turn_head(0)
            phase_slab("o", 3, xnH, xnL)
            numerator(2)
            turn_head(1)
            fill(0)
            numerator(3)
            turn_head(2)
            turn_head(3)


            def out_phase(name, mix0, f, n_norm):
                for i in range(4):
                    phase_slab(name, i, mixH, mixL, ready=(s_mix, mix0) if i == 0 else None)
                fill(f, {1: lambda: norm_sums(n_norm), 6: lambda: norm_spread(n_norm)})

            def mlp(layer, feed, n_norm, f):
                up, down = f"up{layer}", f"down{layer}"
                s0, g0 = SLAB0[up], GROUP0[up]
                d0 = DRAIN[g0][1]
                for j in range(4):
                    phase_slab(up, j, xnH, xnL, ready=(s_xn, 4 * feed) if j == 0 else None)
                    if j == 0:
                        norm(n_norm)
                with pe.Fori(0, 3) as i:
                    for j in range(4):
                        pe.wait_ge(s_drain["V"], i * 4 + (d0 + 4 + j - 2))
                        slab(i * 4 + (s0 + 4 + j), (s0 + j) % HL, slot(g0 + j), xnH, xnL)
                s0, g0 = SLAB0[down], GROUP0[down]
                d0 = DRAIN[g0][1]
                with pe.Fori(0, 2) as i:
                    for j in range(2):
                        slot_free(g0 + j)
                        pe.wait_ge(s_drain["A"], i * 2 + (d0 + j - 2))
                        for kk in range(4):
                            b = s0 + 4 * j + kk
                            slab(i * 8 + b, b % HL, slot(g0 + j), hH, hL, c0=8 * kk, first=kk == 0, last=kk == 3,
                                 ready=(s_hid, 16 * layer + 4 * kk) if j == 0 else None)
                fill(f, {1: lambda: norm_sums(n_norm + 1), 6: lambda: norm_spread(n_norm + 1)})

            pe.wait_ge(s_mixf, NH)
            out_phase("out0", 0, 1, 2)
            mlp(0, 1, 3, 2)

            for i in range(12):
                phase_slab("cin", i, xnH, xnL, ready=(s_xn, 8) if i == 0 else None)
                if i == 0:
                    norm(5)
            fill(3)
            out_phase("out1", 4, 4, 6)
            mlp(1, 3, 7, 5)

            def ret_scores(h):
                pe.wait_ge(s_rqk, 4)
                if h:
                    pe.wait_ge(s_rs, h)
                pe.matmul(pa[:, 0:T], rk[:, h, 0:P], rq[:, h, :], start=True, stop=True)
                pe.matmul(pa[:, T:T + P], rk[:, h, P:T], rq[:, h, P:T], start=True, stop=True).then_inc(s_rS, 1)

            def ret_values(h):
                pe.wait_ge(s_rs, h + 1)
                pe.wait_ge(s_drain["A"], DRAIN[GROUP0["rv"] + 1][1])
                if h >= 2:
                    pe.wait_ge(s_ro, h - 1)
                bank = pc if h % 2 else pb
                pe.matmul(bank[:, 0:T], rv[:, 0, h * RH:(h + 1) * RH], rs[h % 2][:, 0:T], start=True, stop=False)
                pe.matmul(bank[:, P:T], rv[:, 1, h * RH:(h + 1) * RH], rs[h % 2][:, T:T + P], start=False, stop=True)\
                    .then_inc(s_rO, 1)

            def pool_product(j):
                pe.wait_ge(s_pool, j + 1)
                pe.wait_ge(s_rc, 48)
                if j:
                    pe.wait_ge(s_pf, j)
                else:
                    pe.wait_ge(s_rs, NH)
                for e in range(2):
                    mm = pe.matmul(pa[:, e * T:(e + 1) * T], poolwt[:, 2 * j + e, :], pooled[:, e, :], start=True, stop=True)
                mm.then_inc(s_pw, 1)

            for i in range(4):
                phase_slab("rq", i, xnH, xnL, ready=(s_xn, 16) if i == 0 else None)
                if i == 0:
                    norm(9)
            phase_slab("rv", 0, xnH, xnL, by_token=True)
            phase_slab("rv", 1, xnH, xnL, by_token=True)
            ret_scores(0)
            phase_slab("rug", 0, xnH, xnL)
            ret_scores(1)
            ret_values(0)
            phase_slab("rug", 1, xnH, xnL)
            ret_scores(2)
            ret_values(1)
            phase_slab("rug", 2, xnH, xnL)
            ret_scores(3)
            ret_values(2)
            pool_product(0)
            phase_slab("rug", 3, xnH, xnL)
            ret_values(3)
            pool_product(1)
            pe.wait_ge(s_ro, NH)
            pe.wait_ge(s_Rs, 6)
            for h in range(NH):
                for t in range(TT):
                    mm = pe.matmul(pn[:, h * TT + t:h * TT + t + 1], rosq[:, h, t * P:(t + 1) * P], ones[:, 0:1],
                                   start=True, stop=True)
            mm.then_inc(s_rsum, 1)
            fill(6)
            for hp in range(2):
                pe.wait_ge(s_rdiag, hp + 1)
                bank = pc if hp else pb
                for e in range(2):
                    for t in range(TT):
                        mm = pe.matmul(bank[:, e * T + t * P:e * T + (t + 1) * P], ones[:, :], rdiag[:, e, t, :],
                                       start=True, stop=True)
                mm.then_inc(s_rR, 1)
            for i in range(4):
                phase_slab("out2", i, mixH, mixL, ready=(s_mix, 8) if i == 0 else None)

            def xa_scores(h):
                pe.wait_ge(s_drain["V"], DRAIN[GROUP0["wq"] + h][1])
                if h == 0:
                    pe.wait_ge(s_drain["V"], DRAIN[GROUP0["f3"]][1])
                else:
                    pe.wait_ge(s_xe, h)
                for t in range(TT):
                    for c in range(2):
                        mm = pe.matmul(pa[:, t * T:(t + 1) * T], xq[h % 2][:, c, t * P:(t + 1) * P], memk[:, 2 * h + c, :],
                                       start=c == 0, stop=c == 1)
                mm.then_inc(s_xs, 1)

            def xa_turn(h):
                pe.wait_ge(s_xpn, h + 1)
                if h:
                    pe.wait_ge(s_xpT, h)
                for m in range(TT):
                    for t in range(TT):
                        mm = pe.transpose(pb[:, m * T + t * P:m * T + (t + 1) * P], xpn[h % 2][:, t, m * P:(m + 1) * P],
                                          ident[:, :])
                mm.then_inc(s_xT, 1)

            def xa_values(h):
                pe.wait_ge(s_xpT, h + 1)
                if h == 3:
                    pe.wait_ge(s_drain["A"], DRAIN[GROUP0["f7"]][1])
                if h:
                    pe.wait_ge(s_mix, 12 + h)
                for c in range(2):
                    for m in range(TT):
                        mm = pe.matmul(pc[:, c * T:(c + 1) * T], memv[:, m, h * XH + c * P:h * XH + (c + 1) * P],
                                       xpT[h % 2][:, m, :], start=m == 0, stop=m == 1)
                mm.then_inc(s_xo, 1)

            phase_slab("wq", 0, xnH, xnL, ready=(s_xn, 20))
            pe.wait_ge(s_rms, 1)
            norm(10)
            phase_slab("wq", 1, xnH, xnL)
            xa_scores(0)
            phase_slab("wq", 2, xnH, xnL)
            xa_scores(1)
            xa_turn(0)
            phase_slab("wq", 3, xnH, xnL)
            xa_values(0)
            xa_turn(1)
            xa_scores(2)
            fill(7)
            xa_values(1)
            xa_turn(2)
            xa_scores(3)
            xa_values(2)
            xa_turn(3)
            xa_values(3)
            for i in range(4):
                phase_slab("wo", i, mixH, mixL, ready=(s_mix, 12) if i == 0 else None)

            s0, g0 = SLAB0["fup"], GROUP0["fup"]
            d0 = DRAIN[g0][1]
            phase_slab("fup", 0, xnH, xnL, ready=(s_xn, 24))
            norm(11)
            phase_slab("fup", 1, xnH, xnL)
            with pe.Fori(0, (FT // 2 - 2) // 4) as i:
                for j in range(4):
                    pe.wait_ge(s_drain["V"], i * 4 + (d0 + j))
                    slab(i * 4 + (s0 + 2 + j), (s0 + j) % HL, slot(g0 + j), xnH, xnL)
            s0, g0 = SLAB0["fdown"], GROUP0["fdown"]
            for g in range(4):
                slot_free(g0 + g)
                for k in range(FC):
                    for n in range(2):
                        tile = (g * FC + k) * 2 + n
                        s, at_ = s0 + tile // 16, tile % 16
                        if at_ % 8 == 0:
                            weights_ready(s, at_ // 8)
                        if g == 0 and k % 2 == 0 and n == 0:
                            pe.wait_ge(s_f, k // 2 + 1)
                        mm = products(slot(g0 + g), n, s % HL, at_ // 2, hH, hL, k, k == 0, k == FC - 1)
                        if at_ == 15:
                            mm.then_inc(s_slab, 1)
                        elif k == FC - 1 and n == 1:
                            mm.then_inc(s_group, 1)
            norm(12)

        @block.scalar
        def _(act):
            def split(b, i=None, turns=0):
                if i is None and b >= SLABS:
                    return
                loaded = 16 * (b // RAW + 1)
                act.wait_ge(s_raw[b % RAW], loaded if i is None else i * (16 * turns // RAW) + loaded)
                if b >= HL:
                    act.wait_ge(s_slab, b - 1 if i is None else i * turns + (b - 1))
                for half in range(2):
                    hs = slice(half * HALF, (half + 1) * HALF)
                    act.activation(wH[b % HL][:, hs], raw[b % RAW][:, hs], ACT.Copy).then_inc(s_hi, 1)

            chain = [0]

            def link(instruction):
                chain[0] += 1
                instruction.then_inc(s_ach, 1)
                act.wait_ge(s_ach, chain[0])

            def feed_pair(p, gain, ready):
                act.wait_ge(*ready)
                for c in (2 * p, 2 * p + 1):
                    act.activation(xnH[:, c, :], x[:, c, :], ACT.Identity, scale=col(gain, c)).then_inc(s_xnH, 1)
                act.activation(sq[p], x[:, 2 * p:2 * p + 2, :], ACT.Square).then_inc(s_sq, 1)

            def feed(gain, ready):
                for p in range(4):
                    feed_pair(p, gain, ready(p))

            def mem_pair(p):
                act.wait_ge(s_mem, 16)
                act.wait_ge(s_sum, 1)
                for c in (2 * p, 2 * p + 1):
                    act.activation(memH[:, c, :], mem[:, c, :], ACT.Identity, scale=col("gmem", c)).then_inc(s_mmH, 1)
                act.activation(sq[p], mem[:, 2 * p:2 * p + 2, :], ACT.Square).then_inc(s_sq, 1)

            def keep_R(n, dst):
                act.wait_ge(s_R, n + 1)
                act.activation(dst, pn[:, 128:128 + T], ACT.Copy).then_inc(s_Rs, 1)

            def group(name, i):
                act.wait_ge(s_slab, SLAB0[name] + i + 1)
                return slot(GROUP0[name] + i)

            def keep_values(name, i, dst, r, norm_done):
                psum = group(name, i)
                act.wait_ge(s_r, norm_done)
                for t in range(TT):
                    k = act.activation(dst(t), psum[:, t, 0:256], ACT.Identity, scale=r[:, t:t + 1])
                k.then_inc(s_drain["A"], 1)

            def keep_y(psum, g):
                act.activation(squares[:, g, :, :], psum[:, :, 0:T], ACT.Square).then_inc(s_sq, 1)
                act.activation(y[:, g * 2:g * 2 + 2, :] if isinstance(g, int) else y[:, bass.ts(g, 2), :],
                               psum[:, :, 0:T], ACT.Copy).then_inc(s_drain["A"], 1)

            def mix_hi(src, pair, done):
                act.wait_ge(*done)
                act.activation(mixH[:, 2 * pair:2 * pair + 2, :], src, ACT.Copy).then_inc(s_mixH, 1)

            act.wait_ge(s_par, 16)
            for p in range(2):
                feed_pair(p, "g00", (s_x[p], 16))
            split(0)
            for p in range(2, 4):
                feed_pair(p, "g00", (s_x[p], 16))
            split(1)
            split(2)
            keep_R(0, Rs[:, :])
            split(3)
            mem_pair(0)
            act.wait_ge(s_gz, 1)
            act.activation(gt[:, :, :], gz[:, :, :], ACT.Tanh, scale=1.0 / CAP).then_inc(s_gt, 1)
            act.wait_ge(s_gcap, 1)
            link(act.activation(fexp[:, :, :], gcap[:, :, NH:2 * NH], ACT.Exp, scale=-1.0))
            act.activation(softp[:, :, :], fexp[:, :, :], ACT.Ln, bias=1.0).then_inc(s_sp, 1)
            split(4)
            split(5)
            mem_pair(1)
            v0 = SLAB0["v"]

            def keep_vx(h):
                keep_values("v", h, lambda t: vx[:, t, h, 0:VD], rtok, 1)

            def decays(h):
                act.wait_ge(s_darg, h + 1)
                act.activation(dexp[:, 0:T], dargs[:, 0:T], ACT.Exp, bias=av[:, 0, h:h + 1])
                act.activation(dexp[:, T:T + P], dargs[:, T:T + P], ACT.Exp, bias=av[:, 1, h:h + 1]).then_inc(s_dexp, 1)

            def gate_o(i):
                act.wait_ge(s_drain["V"], DRAIN[GROUP0["o"] + i][1])
                act.activation(sigo[:, 2 * i:2 * i + 2, :], sigo[:, 2 * i:2 * i + 2, :], ACT.Sigmoid).then_inc(s_osig, 1)

            def keep_numerator(h):
                act.wait_ge(s_num, h + 1)
                if h:
                    act.wait_ge(s_numk, h)
                if h >= 2:
                    act.wait_ge(s_hn, h - 1)
                for t, bank in enumerate((pc, pb)):
                    act.activation(num[h % 2][:, t, :], bank[:, 0:VD + 1], ACT.Copy)
                    k = act.activation(junk[:, :], bank[:, 0:VD], ACT.Square, accum_out=ssq[:, h, t:t + 1])
                    if t == 0:
                        link(k)
                k.then_inc(s_numk, 1)

            keep_vx(0)
            split(v0 + 2)
            mem_pair(2)
            keep_vx(1)
            split(v0 + 3)
            mem_pair(3)
            act.wait_ge(s_md, 1)
            act.activation(em[:, :, :], mdiff[:, :, :], ACT.Exp).then_inc(s_em, 1)
            decays(0)
            keep_vx(2)
            split(v0 + 4)
            decays(1)
            keep_vx(3)
            split(v0 + 5)
            decays(2)
            split(v0 + 6)
            decays(3)
            gate_o(0)
            split(v0 + 7)
            keep_R(1, Rm[:, :])
            gate_o(1)
            keep_numerator(0)
            split(v0 + 8)
            gate_o(2)
            keep_numerator(1)
            mix_hi(mixf[:, :, :], 0, (s_mixf, 1))
            split(v0 + 9)
            gate_o(3)
            keep_numerator(2)
            mix_hi(mixf[:, :, :], 1, (s_mixf, 2))
            split(v0 + 10)
            keep_numerator(3)
            mix_hi(mixf[:, :, :], 2, (s_mixf, 3))
            mix_hi(mixf[:, :, :], 3, (s_mixf, 4))

            def out_phase(name):
                for i in range(4):
                    keep_y(group(name, i), i)
                    split(SLAB0[name] + i + 2)

            def fill_values(h):
                keep_values(f"f{4 + h}", 0, lambda t: memv[:, t, h * XH:(h + 1) * XH], rmem, 2)

            def mlp(layer, feed_ready, gain, n_norm):
                up, down = f"up{layer}", f"down{layer}"
                s0 = SLAB0[up]
                d0 = DRAIN[GROUP0[up]][1]
                feed(gain, feed_ready)
                if layer == 1:
                    fill_values(0)
                split(s0 + 1)

                def square(n, i=None):
                    def at(v, m=4):
                        return v if i is None else i * m + v
                    act.wait_ge(s_drain["V"], at(d0 + n))
                    act.activation(hsq[n % 2][:, :, :], hrelu[n % 2][:, :, :], ACT.Square).then_inc(s_hs, 1)
                    act.wait_ge(s_hs, at(16 * layer + n + 1))
                    dst = hH[:, 2 * n:2 * n + 2, :] if i is None else hH[:, bass.ts(i * 4 + n, 2), :]
                    act.activation(dst, hsq[n % 2][:, :, :], ACT.Copy).then_inc(s_hidH, 1)

                for n in range(4):
                    split(s0 + n + 2)
                    if n == 0:
                        keep_R(n_norm, Rs[:, :])
                    square(n)
                with act.Fori(0, 3) as i:
                    for j in range(4):
                        split(s0 + 4 + j + 2, i, 4)
                        square(4 + j, i)
                s0 = SLAB0[down]
                with act.Fori(0, 2) as i:
                    for j in range(2):
                        for kk in range(4):
                            b = s0 + 4 * j + kk
                            if kk == 3:
                                act.wait_ge(s_slab, i * 8 + (b + 1))
                                keep_y(slot(GROUP0[down] + j), i * 2 + j)
                            split(b + 2, i, 8)

            after_norm = lambda base: (lambda p: (s_xadd, base + p + 1))
            out_phase("out0")
            mlp(0, after_norm(0), "g02", 3)
            feed("g10", after_norm(4))
            split(SLAB0["cin"] + 1)

            c0 = SLAB0["cin"]
            for i in range(12):
                split(c0 + i + 2)
                if i == 0:
                    keep_R(5, Rs[:, :])
                j = i // 3
                if i % 3 == 0:
                    psum = group("cin", i)
                    if j:
                        act.wait_ge(s_drain["V"], DRAIN[GROUP0["cin"] + i - 2][1])
                    act.activation(csb[:, :, :], psum[:, :, 0:T], ACT.Copy).then_inc(s_drain["A"], 1)
                elif i % 3 == 1:
                    act.wait_ge(s_u, j + 1)
                    for e in range(2):
                        k = act.activation(conv[:, e, :], upad[:, e, 2:], ACT.Identity, scale=col("wconv", 2 * C + 2 * j + e))
                    k.then_inc(s_cv, 1)
                else:
                    mix_hi(cout[:, :, :], j, (s_cf, j + 1))
            split(SLAB0["f3"] + 2)
            out_phase("out1")
            mlp(1, after_norm(8), "g12", 7)
            feed("gmix", after_norm(12))
            fill_values(1)
            split(SLAB0["rq"] + 1)

            r0 = SLAB0["rq"]
            for i in range(4):
                split(r0 + i + 2)
                if i == 0:
                    keep_R(9, Rs[:, :])
                    act.wait_ge(s_trig, 1)
                    act.activation(sint[:, :], ang[:, :], ACT.Sin).then_inc(s_trigd, 1)
                    act.wait_ge(s_trig, 2)
                    act.activation(cost[:, :], turn[:, :], ACT.Sin).then_inc(s_trigd, 1)
                act.wait_ge(s_drain["V"], DRAIN[GROUP0["rq"] + i][1])
                act.activation(rot[0:64, :, :], rop[64:128, :, :], ACT.Copy, scale=-1.0)
                act.activation(rot[64:128, :, :], rop[0:64, :, :], ACT.Copy).then_inc(s_rot, 1)

            def keep_o(h):
                act.wait_ge(s_rO, h + 1)
                bank = pc if h % 2 else pb
                act.activation(ro[:, h, :], bank[:, 0:T], ACT.Copy)
                act.activation(rosq[:, h, :], bank[:, 0:T], ACT.Square).then_inc(s_ro, 1)

            def silu_g(i):
                act.wait_ge(s_drain["V"], DRAIN[GROUP0["rug"] + 2 + i][1])
                act.activation(rsg[:, 2 * i:2 * i + 2, :], rsg[:, 2 * i:2 * i + 2, :], ACT.Silu).then_inc(s_rsg, 1)

            def pool_out(j):
                act.wait_ge(s_pw, j + 1)
                if j:
                    act.wait_ge(s_mix, 8 + j)
                for e in range(2):
                    k = act.activation(yret[:, e, :], pa[:, e * T:(e + 1) * T], ACT.Identity, scale=col("pscale", 2 * j + e))
                k.then_inc(s_pf, 1)
                mix_hi(yret[:, :, :], j, (s_pf, j + 1))

            v0 = SLAB0["rv"]
            for i in range(2):
                keep_values("rv", i, lambda t: rv[:, t, i * 256:(i + 1) * 256], rtok, 10)
                split(v0 + i + 2)
            split(v0 + 4)
            keep_o(0)
            split(v0 + 5)
            keep_o(1)
            split(v0 + 6)
            silu_g(0)
            keep_o(2)
            pool_out(0)
            split(v0 + 7)
            silu_g(1)
            keep_o(3)
            pool_out(1)
            fill_values(2)
            split(v0 + 8)
            for hp in range(2):
                mix_hi(yret[:, :, :], 2 + hp, (s_ry, hp + 1))

            def residual(name):
                return lambda p: (s_drain["V"], DRAIN[GROUP0[name] + p][1])

            for i in range(4):
                split(SLAB0["out2"] + i + 2)
                feed_pair(i, "gxa", residual("out2")(i))

            def softmax(h):
                act.wait_ge(s_xneg, h + 1)
                if h >= 2:
                    act.wait_ge(s_xpn, h - 1)
                for t in range(TT):
                    k = act.activation(xp[h % 2][:, t, :], pa[:, t * T:(t + 1) * T], ACT.Exp, scale=XH ** -0.5,
                                       bias=xneg[:, h, t:t + 1], accum_out=xsum[:, h, t:t + 1])
                k.then_inc(s_xe, 1)

            def xa_hi(h):
                mix_hi(pc[:, :].rearrange("p (a t) -> p a t", a=2), h, (s_xo, h + 1))

            q0 = SLAB0["wq"]
            split(q0 + 2)
            keep_R(10, Rs[:, :])
            split(q0 + 3)
            softmax(0)
            split(q0 + 4)
            softmax(1)
            split(q0 + 5)
            xa_hi(0)
            softmax(2)
            fill_values(3)
            split(q0 + 6)
            xa_hi(1)
            softmax(3)
            xa_hi(2)
            xa_hi(3)
            for i in range(4):
                split(SLAB0["wo"] + i + 2)
                feed_pair(i, "gffn", residual("wo")(i))

            s0, d0 = SLAB0["fup"], DRAIN[GROUP0["fup"]][1]
            side = [cgate, cval]
            wcol, bcol = PCOL["fw"] + 2 * FT, PCOL["fb"]

            def taps(n, i=None):
                def at(v, m=4):
                    return v if i is None else i * m + v
                act.wait_ge(s_drain["V"], at(d0 + n))
                if n >= 2:
                    if n % 2 == 0:
                        act.wait_ge(s_fh, at(n // 2, 2))
                    else:
                        act.wait_ge(s_f, at(n // 2, 2))
                for e in range(2):
                    t = 2 * n + e
                    if i is None:
                        w, b = par[:, wcol + t:wcol + t + 1], par[:, bcol + t:bcol + t + 1]
                    else:
                        w, b = par[:, bass.ts(i * 8 + (wcol + t), 1)], par[:, bass.ts(i * 8 + (bcol + t), 1)]
                    k = act.activation(side[n % 2][:, e, :], apad[n % 2][:, e, 2:], ACT.Identity, scale=w, bias=b)
                k.then_inc(s_fc, 1)

            def behind(n, i=None):
                def at(v, m=4):
                    return v if i is None else i * m + v
                if n % 2 == 0:
                    act.wait_ge(s_fcd, at(2 * n + 2, 8))
                    act.activation(cgate[:, :, :], cgate[:, :, :], ACT.Silu).then_inc(s_fs, 1)
                else:
                    m = n // 2
                    act.wait_ge(s_fh, at(m + 1, 2))
                    dst = hH[:, 2 * m:2 * m + 2, :] if i is None else hH[:, bass.ts(i * 2 + m, 2), :]
                    act.activation(dst, cval[:, :, :], ACT.Copy).then_inc(s_fH, 1)

            split(s0 + 2)
            keep_R(11, Rs[:, :])
            taps(0)
            split(s0 + 3)
            behind(0)
            taps(1)
            with act.Fori(0, (FT // 2 - 2) // 4) as i:
                for j in range(4):
                    split(s0 + 4 + j, i, 4)
                    behind(1 + j, i)
                    taps(2 + j, i)
            s0 = SLAB0["fdown"]
            behind(FT // 2 - 1)
            for s in range(s0 + 2, SLABS):
                split(s)
                for p in range(4):
                    if (44 * (p + 1) - 1) // 16 == s - 2 - s0:
                        act.wait_ge(s_drain["V"], DRAIN[GROUP0["fdown"] + p][1])
                        act.activation(sq[p], x[:, 2 * p:2 * p + 2, :], ACT.Square).then_inc(s_sq, 1)
            act.wait_ge(s_drain["V"], DRAIN[GROUP0["fdown"] + 3][1])
            act.activation(sq[3], x[:, 6:8, :], ACT.Square).then_inc(s_sq, 1)

        @block.vector
        def _(dve):
            chain = [0]

            def link(instruction):
                chain[0] += 1
                instruction.then_inc(s_dch, 1)
                dve.wait_ge(s_dch, chain[0])

            def split(b, i=None, turns=0, halves=(0, 1)):
                if i is None and b >= SLABS:
                    return
                for half in halves:
                    hs = slice(half * HALF, (half + 1) * HALF)
                    dve.wait_ge(s_hi, 2 * b + half + 1 if i is None else i * (2 * turns) + (2 * b + half + 1))
                    dve.tensor_tensor(wL[b % HL][:, hs], raw[b % RAW][:, hs], wH[b % HL][:, hs].bitcast(f32), ALU.subtract)\
                        .then_inc(s_lo, 1)

            def feed(n, gain):
                for c in range(C):
                    dve.wait_ge(s_xnH, C * n + c + 1)
                    k = dve.scalar_tensor_tensor(xnL[:, c, :], x[:, c, :], col(gain, c), xnH[:, c, :].bitcast(f32),
                                                 ALU.mult, ALU.subtract)
                    if c % 2:
                        k.then_inc(s_xn, 1)

            def feed_pair(n, p, gain):
                for c in (2 * p, 2 * p + 1):
                    dve.wait_ge(s_xnH, C * n + c + 1)
                    k = dve.scalar_tensor_tensor(xnL[:, c, :], x[:, c, :], col(gain, c), xnH[:, c, :].bitcast(f32),
                                                 ALU.mult, ALU.subtract)
                k.then_inc(s_xn, 1)

            def mem_pair(p):
                for c in (2 * p, 2 * p + 1):
                    dve.wait_ge(s_mmH, c + 1)
                    k = dve.scalar_tensor_tensor(memL[:, c, :], mem[:, c, :], col("gmem", c), memH[:, c, :].bitcast(f32),
                                                 ALU.mult, ALU.subtract)
                k.then_inc(s_mm, 1)

            def mean_square(n):
                dve.wait_ge(s_sum, n + 1)
                dve.tensor_scalar(ms[:, :], pn[:, 0:TT], 1.0 / D, EPS, ALU.mult, ALU.add).then_inc(s_ms, 1)

            def diagonal(n):
                r = rmem if n == 1 else rtok
                dve.wait_ge(s_r, n + 1)
                for t in range(TT):
                    k = dve.tensor_scalar(diag[:, t, :], ident[:, :], r[:, t:t + 1], None, ALU.mult)
                k.then_inc(s_diag, 1)

            def group(name, i):
                dve.wait_ge(s_slab, SLAB0[name] + i + 1)
                return slot(GROUP0[name] + i)

            def keep(name, i, dst, R=None):
                psum = group(name, i)
                dve.tensor_tensor(dst, psum[:, :, 0:T], over_pair(Rs[:, :] if R is None else R), ALU.mult)\
                    .then_inc(s_drain["V"], 1)

            def mix_lo(src, pair, n):
                dve.wait_ge(s_mixH, n + 1)
                dve.tensor_tensor(mixL[:, 2 * pair:2 * pair + 2, :], src, mixH[:, 2 * pair:2 * pair + 2, :].bitcast(f32),
                                  ALU.subtract).then_inc(s_mix, 1)

            dve.memset(ones[:, :], 1.0)
            dve.memset(minus_half[:, :], -0.5)
            dve.memset(mrow[0][:, 0:P], 0.0)
            dve.memset(mrow[1][:, 0:P], 0.0)
            dve.memset(vx[:, :, :, VD:VD + 1], 1.0).then_inc(s_set, 1)

            dve.wait_ge(s_par, 16)
            feed_pair(0, 0, "g00")
            feed_pair(0, 1, "g00")
            split(0)
            feed_pair(0, 2, "g00")
            feed_pair(0, 3, "g00")
            split(1)
            dve.wait_ge(s_cst, 80)
            dve.tensor_tensor(wgs[:, :, :], wg[:, :, :],
                              col("g00", 0, C).rearrange("p (c o) -> p c o", o=1).to_broadcast([P, C, 2 * NH]), ALU.mult)\
                .then_inc(s_wgs, 1)
            mean_square(0)
            diagonal(0)
            split(2)
            dve.wait_ge(s_Rs, 1)
            keep("qk", 0, qT[:, 0:2, :])
            split(3)
            keep("qk", 1, qT[:, 2:4, :])
            mem_pair(0)
            dve.wait_ge(s_gates, 1)
            for t in range(TT):
                k = dve.scalar_tensor_tensor(gz[:, t, :], pa[:, t * 8:t * 8 + 8], rtok[:, t:t + 1], col("bgates", 0, 2 * NH),
                                             ALU.mult, ALU.add)
            k.then_inc(s_gz, 1)
            dve.wait_ge(s_gt, 1)
            dve.tensor_scalar(gcap[:, :, :], gt[:, :, :], CAP, None, ALU.mult).then_inc(s_gcap, 1)
            split(4)
            keep("qk", 2, kT[:, 0:2, :])
            split(5)
            keep("qk", 3, kT[:, 2:4, :])
            dve.wait_ge(s_cum, 1)
            sums = pa[:, 0:TT * NH].rearrange("p (t h) -> p t h", t=TT)
            dve.tensor_copy(nb[:, :, :], sums)
            dve.wait_ge(s_gcap, 1)
            dve.tensor_tensor(av[:, :, :], gcap[:, :, 0:NH], sums, ALU.add).then_inc(s_av, 1)
            mem_pair(1)
            dve.wait_ge(s_avT, 1)
            link(dve.tensor_scalar(mrow[0][:, P:], pb[0:NH, 0:T], 0.0, None, ALU.max))
            a, back = 0, 1
            while back < T:
                k = dve.tensor_tensor(mrow[1 - a][:, P:], mrow[a][:, P:], mrow[a][:, P - back:P - back + T], ALU.max)
                a, back = 1 - a, 2 * back
                if back < T:
                    link(k)
                else:
                    k.then_inc(s_mrow, 1)
            assert a == 0
            split(6)
            mem_pair(2)
            dve.wait_ge(s_mT, 1)
            dve.tensor_tensor(mdiff[:, :, :], nb[:, :, :], pc[:, 0:TT * NH].rearrange("p (t h) -> p t h", t=TT), ALU.subtract)\
                .then_inc(s_md, 1)
            split(7)
            mem_pair(3)

            def exponents(h):
                dve.wait_ge(s_S, h + 1)
                if h:
                    dve.wait_ge(s_dexp, h)
                dve.tensor_tensor(dargs[:, 0:T], maskt[:, :], pb[:, 0:T], ALU.subtract)
                dve.tensor_tensor(dargs[:, T:T + P], maskt[:, 0:P], pb[:, P:T], ALU.subtract).then_inc(s_darg, 1)

            def probabilities(h):
                dve.wait_ge(s_dexp, h + 1)
                dve.scalar_tensor_tensor(prob[h][:, :], pa[:, 0:T + P], QK ** -0.5, dexp[:, :], ALU.mult, ALU.mult)\
                    .then_inc(s_P, 1)

            def normalise(h):
                dve.wait_ge(s_numk, h + 1)
                dve.wait_ge(s_em, 1)
                sums = num[h % 2][:, :, VD:VD + 1].rearrange("p t o -> p (t o)")
                link(dve.scalar_tensor_tensor(den[:, h, :], sums, -1.0, sums, ALU.mult, ALU.max))
                link(dve.tensor_tensor(den[:, h, :], den[:, h, :], em[:, :, h:h + 1].rearrange("p t o -> p (t o)"), ALU.max))
                link(dve.reciprocal(rec[:, h, :], den[:, h, :]))
                link(dve.tensor_tensor(rec2[:, h, :], rec[:, h, :], rec[:, h, :], ALU.mult))
                link(dve.scalar_tensor_tensor(hms[:, h, :], ssq[:, h, :], 1.0 / VD, rec2[:, h, :], ALU.mult, ALU.mult))
                dve.tensor_scalar(hms[:, h, :], hms[:, h, :], EPS, None, ALU.add).then_inc(s_hms, 1)
                dve.wait_ge(s_hr, h + 1)
                link(dve.tensor_tensor(hc[:, h, :], rec[:, h, :], hr[:, h, :], ALU.mult))
                if h >= 2:
                    dve.wait_ge(s_hT, h - 1)
                for t in range(TT):
                    k = dve.tensor_scalar(hn[h % 2][:, t, :], num[h % 2][:, t, 0:VD], hc[:, h, t:t + 1], None, ALU.mult)
                k.then_inc(s_hn, 1)

            def gated(h):
                dve.wait_ge(s_hT, h + 1)
                dve.wait_ge(s_osig, h + 1)
                if h:
                    dve.wait_ge(s_mix, h)
                for e in range(2):
                    k = dve.scalar_tensor_tensor(mixf[:, e, :], pn[:, e * T:(e + 1) * T], col("ghn", 2 * h + e),
                                                 sigo[:, 2 * h + e, :], ALU.mult, ALU.mult)
                k.then_inc(s_mixf, 1)

            def keep_o(i):
                keep("o", i, sigo[:, 2 * i:2 * i + 2, :])

            exponents(0)
            split(8)
            probabilities(0)
            exponents(1)
            split(9)
            probabilities(1)
            exponents(2)
            split(10)
            probabilities(2)
            keep_o(0)
            exponents(3)
            probabilities(3)
            split(11)
            mean_square(1)
            keep_o(1)
            diagonal(1)
            split(12)
            normalise(0)
            keep_o(2)
            normalise(1)
            gated(0)
            mix_lo(mixf[:, :, :], 0, 0)
            split(13)
            keep_o(3)
            normalise(2)
            gated(1)
            mix_lo(mixf[:, :, :], 1, 1)
            split(14)

            def fill_keys(h):
                dve.wait_ge(s_Rs, 2)
                keep(f"f{h}", 0, memk[:, 2 * h:2 * h + 2, :], Rm[:, :])

            fill_keys(0)
            normalise(3)
            gated(2)
            mix_lo(mixf[:, :, :], 2, 2)
            gated(3)
            mix_lo(mixf[:, :, :], 3, 3)

            def update(n, gain):
                dve.wait_ge(s_R, n + 1)
                for c in range(C):
                    k = dve.scalar_tensor_tensor(y[:, c, :], y[:, c, :], col(gain, c), pn[:, 128:128 + T], ALU.mult, ALU.mult)
                    if c % 2:
                        k.then_inc(s_t, 1)

            def boundary(n, next_slab, post_gain, feeds, pre_gain, filler=None):
                mean_square(n)
                split(next_slab, halves=(0,))
                diagonal(n)
                split(next_slab, halves=(1,))
                update(n, post_gain)
                feed(feeds, pre_gain)
                if filler is not None:
                    fill_keys(filler)
                split(next_slab + 1)

            def out_phase(name):
                for i in range(3):
                    split(SLAB0[name] + i + 2)

            def mlp(layer, n_norm):
                up, down = f"up{layer}", f"down{layer}"
                s0 = SLAB0[up]

                def hidden(n, i=None):
                    dve.wait_ge(s_hidH, 16 * layer + n + 1 if i is None else i * 4 + (16 * layer + n + 1))
                    hs = slice(2 * n, 2 * n + 2) if i is None else bass.ts(i * 4 + n, 2)
                    dve.tensor_tensor(hL[:, hs, :], hsq[n % 2][:, :, :], hH[:, hs, :].bitcast(f32), ALU.subtract)\
                        .then_inc(s_hid, 1)

                def relu(n, i=None):
                    dve.wait_ge(s_slab, s0 + n + 1 if i is None else i * 4 + (s0 + n + 1))
                    dve.scalar_tensor_tensor(hrelu[n % 2][:, :, :], slot(GROUP0[up] + n)[:, :, 0:T], 0.0, over_pair(Rs[:, :]),
                                             ALU.max, ALU.mult).then_inc(s_drain["V"], 1)

                for n in range(4):
                    if n == 0:
                        mean_square(n_norm)
                        diagonal(n_norm)
                        dve.wait_ge(s_Rs, kept_before(n_norm)[0] + 1)
                    relu(n)
                    split(s0 + n + 2)
                    hidden(n)
                with dve.Fori(0, 3) as i:
                    for j in range(4):
                        relu(4 + j, i)
                        split(s0 + 4 + j + 2, i, 4)
                        hidden(4 + j, i)
                s0 = SLAB0[down]
                for kk in range(7):
                    split(s0 + kk + 2)
                with dve.Fori(0, 1) as i:
                    for kk in range(8):
                        split(s0 + 7 + kk + 2, i, 8)

            out_phase("out0")
            boundary(2, SLAB0["up0"], "g01", 1, "g02", filler=1)
            mlp(0, 3)
            boundary(4, SLAB0["cin"], "g03", 2, "g10", filler=2)

            c0 = SLAB0["cin"]
            mean_square(5)
            diagonal(5)
            dve.wait_ge(s_Rs, kept_before(5)[0] + 1)
            dve.tensor_tensor(R2[:, :], Rs[:, :], Rs[:, :], ALU.mult)
            for e in range(2):
                k = dve.memset(upad[:, e, 0:2], 0.0)
            link(k)
            for i in range(12):
                j = i // 3
                if i % 3 == 1:
                    psum = group("cin", i)
                    dve.wait_ge(s_drain["A"], DRAIN[GROUP0["cin"] + i - 1][1])
                    if j:
                        dve.wait_ge(s_u, j)
                    dve.tensor_tensor(cx[:, :, :], psum[:, :, 0:T], csb[:, :, :], ALU.mult).then_inc(s_drain["V"], 1)
                    dve.wait_ge(s_drain["V"], DRAIN[GROUP0["cin"] + i][1])
                    dve.tensor_tensor(upad[:, :, 2:], cx[:, :, :], over_pair(R2[:, :]), ALU.mult).then_inc(s_u, 1)
                if i % 3 == 2:
                    if j:
                        dve.wait_ge(s_cf, j)
                    keep("cin", i, bsb[:, :, :])
                split(c0 + i + 2)
                if i % 3 == 1:
                    dve.wait_ge(s_cv, j + 1)
                    for tap in (1, 0):
                        for e in range(2):
                            k = dve.scalar_tensor_tensor(conv[:, e, :], upad[:, e, tap:tap + T], col("wconv", tap * C + 2 * j + e),
                                                         conv[:, e, :], ALU.mult, ALU.add)
                        link(k)
                if i % 3 == 2:
                    dve.wait_ge(s_drain["V"], DRAIN[GROUP0["cin"] + i][1])
                    if j:
                        dve.wait_ge(s_mix, 4 + j)
                    dve.tensor_tensor(cout[:, :, :], bsb[:, :, :], conv[:, :, :], ALU.mult).then_inc(s_cf, 1)
                    mix_lo(cout[:, :, :], j, 4 + j)
            fill_keys(3)
            split(SLAB0["f3"] + 2)
            out_phase("out1")
            boundary(6, SLAB0["up1"], "g11", 3, "g12")
            mlp(1, 7)
            boundary(8, SLAB0["rq"], "g13", 4, "gmix")

            for t in (upl[:, :, 0:PADW], sl[0][:, 0:PADW], sl[1][:, 0:PADW]):
                dve.memset(t, 0.0)
            dve.memset(halfpi[:, :], math.pi / 2)
            dve.wait_ge(s_pos, 32)
            link(dve.tensor_copy(ang[:, :], posi[:, :]))
            link(dve.tensor_scalar(ang[:, :], ang[:, :], freqt[:, 0:1], None, ALU.mult))
            two_pi = 2 * math.pi
            big = 1.5 * 2.0 ** 23
            part1 = 6.28125
            part2 = 0.0019350051879882812
            part3 = two_pi - part1 - part2

            def reduced(dst, turns):
                link(dve.tensor_scalar(dst, ang[:, :], 1 / two_pi, turns, ALU.mult, ALU.add))
                link(dve.tensor_scalar(dst, dst, big, None, ALU.add))
                link(dve.tensor_scalar(dst, dst, big, None, ALU.subtract))

            reduced(turn[:, :], 0.25)
            reduced(sint[:, :], 0.0)
            link(dve.scalar_tensor_tensor(cost[:, :], turn[:, :], -part1, ang[:, :], ALU.mult, ALU.add))
            link(dve.scalar_tensor_tensor(cost[:, :], turn[:, :], -part2, cost[:, :], ALU.mult, ALU.add))
            link(dve.scalar_tensor_tensor(turn[:, :], turn[:, :], -part3, cost[:, :], ALU.mult, ALU.add))
            link(dve.tensor_scalar(turn[:, :], turn[:, :], math.pi / 2, 3.1415925, ALU.add, ALU.min))
            link(dve.tensor_scalar(turn[:, :], turn[:, :], -3.1415925, None, ALU.max))
            link(dve.scalar_tensor_tensor(ang[:, :], sint[:, :], -part1, ang[:, :], ALU.mult, ALU.add))
            link(dve.scalar_tensor_tensor(ang[:, :], sint[:, :], -part2, ang[:, :], ALU.mult, ALU.add))
            link(dve.scalar_tensor_tensor(ang[:, :], sint[:, :], -part3, ang[:, :], ALU.mult, ALU.add))
            dve.tensor_scalar(ang[:, :], ang[:, :], 3.1415925, -3.1415925, ALU.min, ALU.max).then_inc(s_trig, 2)
            mean_square(9)
            diagonal(9)
            dve.wait_ge(s_Rs, kept_before(9)[0] + 1)
            r0 = SLAB0["rq"]
            for i in range(4):
                if i:
                    dve.wait_ge(s_rot, i)
                keep("rq", i, rop[:, :, :])
                dve.wait_ge(s_drain["V"], DRAIN[GROUP0["rq"] + i][1])
                if i == 0:
                    dve.wait_ge(s_trigd, 2)
                dst = (rq if i < 2 else rk)[:, 2 * (i % 2):2 * (i % 2) + 2, :]
                dve.tensor_tensor(ropc[:, :, :], rop[:, :, :], over_pair(cost[:, :]), ALU.mult)
                split(r0 + i + 2)
                dve.wait_ge(s_rot, i + 1)
                link(dve.tensor_tensor(rops[:, :, :], rot[:, :, :], over_pair(sint[:, :]), ALU.mult))
                dve.tensor_tensor(dst, ropc[:, :, :], rops[:, :, :], ALU.add).then_inc(s_rqk, 1)

            def decayed(h):
                dve.wait_ge(s_rS, h + 1)
                dve.wait_ge(s_rc, 48)
                if h >= 2:
                    dve.wait_ge(s_rO, h - 1)
                dve.tensor_tensor(rs[h % 2][:, 0:T], pa[:, 0:T], decayt[:, h, :], ALU.mult)
                dve.tensor_tensor(rs[h % 2][:, T:T + P], pa[:, T:T + P], decayt[:, h, 0:P], ALU.mult).then_inc(s_rs, 1)

            v0 = SLAB0["rv"]
            split(v0 + 2)
            split(v0 + 3)
            decayed(0)
            keep("rug", 0, upl[:, :, PADW:])
            split(v0 + 4)
            decayed(1)
            dve.wait_ge(s_pool, 1)
            keep("rug", 1, upl[:, :, PADW:])
            split(v0 + 5)
            decayed(2)
            keep("rug", 2, rsg[:, 0:2, :])
            split(v0 + 6)
            decayed(3)
            mix_lo(yret[:, :, :], 0, 8)
            keep("rug", 3, rsg[:, 2:4, :])
            split(v0 + 7)
            mix_lo(yret[:, :, :], 1, 9)
            dve.wait_ge(s_rsum, 1)
            dve.tensor_scalar(rms8[:, :, :], pn[:, 0:NH * TT].rearrange("p (h t) -> p h t", h=NH), 1.0 / RH, EPS, ALU.mult,
                              ALU.add).then_inc(s_rms, 1)
            dve.wait_ge(s_rr, 1)

            def ret_diagonal(hp):
                if hp:
                    dve.wait_ge(s_rR, hp)
                for e in range(2):
                    for t in range(TT):
                        k = dve.tensor_scalar(rdiag[:, e, t, :], ident[:, :], rr8[:, 2 * hp + e, t:t + 1], None, ALU.mult)
                k.then_inc(s_rdiag, 1)

            def ret_out(hp):
                bank = pc if hp else pb
                dve.wait_ge(s_ro, NH)
                for e in range(2):
                    k = dve.scalar_tensor_tensor(ro[:, 2 * hp + e, :], ro[:, 2 * hp + e, :], col("gret", 2 * hp + e),
                                                 bank[:, e * T:(e + 1) * T], ALU.mult, ALU.mult)
                link(k)
                dve.wait_ge(s_rsg, hp + 1)
                dve.tensor_tensor(yret[:, :, :], ro[:, 2 * hp:2 * hp + 2, :], rsg[:, 2 * hp:2 * hp + 2, :], ALU.mult)\
                    .then_inc(s_ry, 1)
                mix_lo(yret[:, :, :], 2 + hp, 10 + hp)

            ret_diagonal(0)
            split(v0 + 8)
            dve.wait_ge(s_rR, 1)
            ret_diagonal(1)
            ret_out(0)
            dve.wait_ge(s_rR, 2)
            ret_out(1)

            def residual(name, i):
                psum = group(name, i)
                dve.tensor_tensor(x[:, 2 * i:2 * i + 2, :], x[:, 2 * i:2 * i + 2, :], psum[:, :, 0:T], ALU.add)\
                    .then_inc(s_drain["V"], 1)

            for i in range(4):
                residual("out2", i)
                split(SLAB0["out2"] + i + 2)
                feed_pair(5, i, "gxa")

            def row_max(h):
                dve.wait_ge(s_xs, h + 1)
                for t in range(TT):
                    k = dve.reduce_max(xmax[:, h, t:t + 1], pa[:, t * T:(t + 1) * T], AX.X)
                link(k)
                dve.tensor_scalar(xneg[:, h, :], xmax[:, h, :], -(XH ** -0.5), None, ALU.mult).then_inc(s_xneg, 1)

            def row_norm(h):
                dve.wait_ge(s_xe, h + 1)
                link(dve.reciprocal(xrec[:, h, :], xsum[:, h, :]))
                if h >= 2:
                    dve.wait_ge(s_xT, h - 1)
                for t in range(TT):
                    k = dve.tensor_scalar(xpn[h % 2][:, t, :], xp[h % 2][:, t, :], xrec[:, h, t:t + 1], None, ALU.mult)
                k.then_inc(s_xpn, 1)

            def keep_turned(h):
                dve.wait_ge(s_xT, h + 1)
                if h >= 2:
                    dve.wait_ge(s_xo, h - 1)
                dve.tensor_copy(xpT[h % 2][:, :, :], pb[:, :].rearrange("p (m t) -> p m t", m=TT)).then_inc(s_xpT, 1)

            def keep_query(h):
                psum = group("wq", h)
                if h >= 2:
                    dve.wait_ge(s_xs, h - 1)
                dve.tensor_tensor(xq[h % 2][:, :, :], psum[:, :, 0:T], over_pair(Rs[:, :]), ALU.mult).then_inc(s_drain["V"], 1)

            def xa_lo(h):
                mix_lo(pc[:, :].rearrange("p (a t) -> p a t", a=2), h, 12 + h)

            q0 = SLAB0["wq"]
            mean_square(10)
            diagonal(10)
            split(q0 + 2)
            dve.wait_ge(s_Rs, kept_before(10)[0] + 1)
            keep_query(0)
            split(q0 + 3)
            keep_query(1)
            row_max(0)
            split(q0 + 4)
            row_norm(0)
            keep_query(2)
            row_max(1)
            keep_turned(0)
            split(q0 + 5)
            row_norm(1)
            keep_query(3)
            keep_turned(1)
            xa_lo(0)
            row_max(2)
            row_norm(2)
            split(q0 + 6)
            xa_lo(1)
            keep_turned(2)
            row_max(3)
            row_norm(3)
            xa_lo(2)
            keep_turned(3)
            xa_lo(3)
            for i in range(4):
                residual("wo", i)
                split(SLAB0["wo"] + i + 2)
                feed_pair(6, i, "gffn")

            s0, d0 = SLAB0["fup"], DRAIN[GROUP0["fup"]][1]
            side = [cgate, cval]

            def scaled(n, i=None):
                def at(v):
                    return v if i is None else i * 4 + v
                dve.wait_ge(s_slab, at(s0 + n + 1))
                dve.tensor_tensor(apad[n % 2][:, :, 2:], slot(GROUP0["fup"] + n)[:, :, 0:T], over_pair(Rs[:, :]), ALU.mult)\
                    .then_inc(s_drain["V"], 1)

            def convolve(n, i=None):
                def at(v, m=4):
                    return v if i is None else i * m + v
                dve.wait_ge(s_fc, at(n + 1))
                for tap in (1, 0):
                    for e in range(2):
                        t = PCOL["fw"] + tap * FT + 2 * n + e
                        w = par[:, t:t + 1] if i is None else par[:, bass.ts(i * 8 + t, 1)]
                        c = side[n % 2][:, e, :]
                        k = dve.scalar_tensor_tensor(c, apad[n % 2][:, e, tap:tap + T], w, c, ALU.mult, ALU.add)
                    k.then_inc(s_fcd, 1)
                    if tap:
                        dve.wait_ge(s_fcd, at(2 * n + 1, 8))

            mean_square(11)
            diagonal(11)
            for a in apad:
                k = dve.memset(a[:, :, 0:2], 0.0)
            link(k)
            split(s0 + 2)
            dve.wait_ge(s_Rs, kept_before(11)[0] + 1)
            scaled(0)
            convolve(0)
            scaled(1)
            split(s0 + 3)
            convolve(1)
            with dve.Fori(0, (FT // 2 - 2) // 4) as i:
                for j in range(4):
                    scaled(2 + j, i)
                    split(s0 + 4 + j, i, 4)
                    convolve(2 + j, i)
            s0 = SLAB0["fdown"]
            for s in range(s0 + 2, SLABS + 2):
                split(s)
                for p in range(4):
                    if (44 * (p + 1) - 1) // 16 == s - 2 - s0:
                        if p < 3:
                            dve.wait_ge(s_group, p + 1)
                        else:
                            dve.wait_ge(s_slab, SLABS)
                        xs = x[:, 2 * p:2 * p + 2, :]
                        dve.tensor_tensor(xs, xs, slot(GROUP0["fdown"] + p)[:, :, 0:T], ALU.add).then_inc(s_drain["V"], 1)
            mean_square(12)
            diagonal(12)
            dve.wait_ge(s_R, 13)
            for c in range(C):
                k = dve.scalar_tensor_tensor(y[:, c, :], x[:, c, :], col("gfin", c), pn[:, 128:128 + T], ALU.mult, ALU.mult)
                if c % 2:
                    k.then_inc(s_outv, 1)

        @block.gpsimd
        def _(pool):
            chain = [0]

            def link(instruction):
                chain[0] += 1
                instruction.then_inc(s_pch, 1)
                pool.wait_ge(s_pch, chain[0])

            def add_squares(n):
                for p in (1, 2):
                    pool.wait_ge(s_sq, 4 * n + p + 1)
                    if p == 2:
                        pool.wait_ge(s_sqa, 2 * n + 1)
                    pool.tensor_tensor(sq[0], sq[0], sq[p], ALU.add).then_inc(s_sqa, 1)

            def factor(n):
                r = rmem if n == 1 else rtok
                pool.wait_ge(s_ms, n + 1)
                pool.tensor_tensor(r[:, :], ms[:, :], minus_half[:, 0:TT], ALU.pow).then_inc(s_r, 1)

            def norm(n):
                add_squares(n)
                factor(n)

            def add_to_x(n):
                for p in range(4):
                    pool.wait_ge(s_t, 4 * n + p + 1)
                    xs = x[:, 2 * p:2 * p + 2, :]
                    pool.tensor_tensor(xs, xs, y[:, 2 * p:2 * p + 2, :], ALU.add).then_inc(s_xadd, 1)

            pool.wait_ge(s_set, 1)
            norm(0)
            norm(1)
            for h in range(NH):
                pool.wait_ge(s_hms, h + 1)
                pool.tensor_tensor(hr[:, h, :], hms[:, h, :], minus_half[:, 0:TT], ALU.pow).then_inc(s_hr, 1)
            for post in range(4):
                norm(2 + 2 * post)
                add_to_x(post)
                norm(3 + 2 * post)
            for j in range(2):
                pool.wait_ge(s_drain["V"], DRAIN[GROUP0["rug"] + j][1])
                if j:
                    pool.wait_ge(s_pw, j)
                pool.wait_ge(s_rc, 48)
                for e in range(2):
                    w = WINDOWS[2 * j + e]
                    src, back, k = upl[:, e, :], 1, 0
                    while back < w:
                        link(pool.tensor_tensor(sl[k][:, PADW:], src[:, PADW:], src[:, PADW - back:PADW - back + T], ALU.add))
                        src, back, k = sl[k], 2 * back, 1 - k
                    pool.tensor_tensor(pooled[:, e, 0:16], src[:, PADW:PADW + 16], recountt[:, 2 * j + e, :], ALU.mult)
                    link(pool.tensor_scalar(pooled[:, e, 16:], src[:, PADW + 16:], 1.0 / w, None, ALU.mult))
                k = pool.tensor_tensor(pooled[:, :, :], pooled[:, :, :], upl[:, :, PADW:], ALU.subtract)
                k.then_inc(s_pool, 1)
            pool.wait_ge(s_rms, 1)
            pool.tensor_tensor(rr8[:, :, :].rearrange("p h t -> p (h t)"), rms8[:, :, :].rearrange("p h t -> p (h t)"),
                               minus_half[:, :], ALU.pow).then_inc(s_rr, 1)
            norm(10)
            norm(11)

            def product(m, i=None):
                def at(v, k=2):
                    return v if i is None else i * k + v
                hs = slice(2 * m, 2 * m + 2) if i is None else bass.ts(i * 2 + m, 2)
                pool.wait_ge(s_fs, at(m + 1))
                pool.wait_ge(s_fcd, at(4 * m + 4, 8))
                pool.tensor_tensor(cval[:, :, :], cgate[:, :, :], cval[:, :, :], ALU.mult).then_inc(s_fh, 1)
                pool.wait_ge(s_fH, at(m + 1))
                pool.tensor_tensor(hL[:, hs, :], cval[:, :, :], hH[:, hs, :].bitcast(f32), ALU.subtract).then_inc(s_f, 1)

            product(0)
            with pool.Fori(0, (FT // 4 - 1) // 2) as i:
                for j in range(2):
                    product(1 + j, i)
            norm(12)


def _slabs(w, by=8):
    k, n = w.shape
    a = w.reshape(k // (by * P), by, P, n // 256, 256).transpose(3, 0, 2, 1, 4)
    return a.reshape(-1, P, SLAB)


def _stream(w):
    k, n = w.shape
    a = w.reshape(k // P, P, n // 256, 2, P).transpose(2, 0, 3, 1, 4).reshape(-1, 16, P, P)
    return a.transpose(0, 2, 1, 3).reshape(-1, P, SLAB)


def _lay_out(v):
    f = {k: np.asarray(a) for k, a in v.items()}
    cat = np.concatenate
    wi = f["w_in_mlstm"][0]
    q, k, vv, o, g = np.split(wi, [NH * QK, 2 * NH * QK, 2 * NH * QK + D, 2 * NH * QK + 2 * D], axis=1)
    fill_k, fill_v = _slabs(f["xa_wkv_2"][0][:, :D]), _slabs(f["xa_wkv_2"][0][:, D:])
    b, c, xh = (_slabs(a) for a in np.split(f["w_in_conv"][0], 3, axis=1))
    cin = np.stack([c, xh, b], axis=1).reshape(-1, P, SLAB)
    i2 = f["w_in_2"][0]
    rqk, rv, rg, ru = i2[:, :2 * RW], i2[:, 2 * RW:3 * RW], i2[:, 3 * RW:4 * RW], i2[:, 4 * RW:]
    wo2 = f["w_out_2"][0]
    gate, val = (_slabs(a) for a in np.split(f["ffn_w_up_2"][0], 2, axis=1))
    weights = cat([
        _slabs(q), _slabs(k), _slabs(vv), _slabs(o), fill_k[0:1],
        _slabs(f["w_out_mlstm"][0]), fill_k[1:2], _slabs(f["w_mlp_up"][0]), _slabs(f["w_mlp_down"][0]), fill_k[2:3],
        cin, fill_k[3:4], _slabs(f["w_out_conv"][0]), fill_v[0:1],
        _slabs(f["w_mlp_up"][1]), _slabs(f["w_mlp_down"][1]), fill_v[1:2],
        _slabs(rqk), _slabs(rv), _slabs(ru), _slabs(rg), fill_v[2:3],
        _slabs(cat([wo2[RW:], wo2[:RW]])), _slabs(f["xa_wq_2"][0]), fill_v[3:4], _slabs(f["xa_wo_2"][0]),
        np.stack([gate, val], axis=1).reshape(-1, P, SLAB), _stream(f["ffn_w_down_2"][0])])

    def cols(a):
        return a.reshape(-1, P).T

    def paired(a):
        return a.reshape(2, -1, 2, P).transpose(1, 0, 2, 3).reshape(-1, P).T

    ng = f["norm_g"]
    params = cat([cols(ng[i, j]) for i in range(2) for j in range(4)] + [
        cols(f["g_hnorm"][0]), cols(f["w_conv"][0]), cols(f["mix_norm_g_2"][0]), cols(f["ret_gn_g_2"][0]),
        cols(f["pool_scale_2"][0]), cols(f["xa_norm_g_2"][0]), cols(f["mem_norm_g_2"]), cols(f["ffn_norm_g_2"][0])]
        + [paired(f["ffn_conv_w_2"][0, i]) for i in range(3)] + [
        paired(f["ffn_conv_b_2"][0]), cols(f["final_norm_g_2"]), np.broadcast_to(f["b_gates_mlstm"][0], (P, 2 * NH))], axis=1)

    def chunks(a):
        return a.reshape(-1, P, a.shape[-1]).transpose(1, 0, 2)

    s, l = np.arange(P)[:, None], np.arange(T)[None, :]
    tri = np.stack([(s <= l[:, :P]).astype(np.float32), np.eye(P, dtype=np.float32)])
    mask = np.where(s <= l, 0.0, BLOCKED).astype(np.float32)
    select = np.zeros((NH, NH, P), np.float32)
    for h in range(NH):
        select[h, h] = 1.0
    lg = np.log1p(-np.exp2(-5.0 - np.arange(NH)))
    decay = np.where(s[:, None] <= l[None], np.exp(lg[None, :, None] * np.maximum(l[None] - s[:, None], 0)), 0.0) * RH ** -0.5
    half = np.arange(0, RH, 2, dtype=np.float32)
    freq = np.exp(np.float32(-math.log(ROPE_BASE)) * half / np.float32(RH)).astype(np.float32)
    freq = np.tile(freq, 2)[:, None]
    recount = np.stack([1.0 / np.minimum(np.arange(1, 17), w) for w in WINDOWS]).astype(np.float32)
    return {
        "xT": chunks(f["x"][0].T), "memT": chunks(f["mem_2"][0].T), "pos": f["positions_2"][0], "weights": weights,
        "wgate": chunks(g), "params": params, "poolw": f["pool_w_2"][0].transpose(1, 0, 2), "tri": tri, "mask": mask,
        "select": select, "decay": decay.astype(np.float32), "freq": freq,
        "recount": np.broadcast_to(recount, (P, NH, 16)),
    }


def kernel(**inputs):
    import concourse.bacc as bacc
    from concourse.bass_utils import run_bass_kernel_spmd

    nc = bacc.Bacc("TRN2", target_bir_lowering=False, num_devices=1)
    arrays, args = {}, []
    for name, a in _lay_out(inputs).items():
        a = np.ascontiguousarray(a)
        arrays[f"in_{name}"] = a
        args.append(nc.dram_tensor(f"in_{name}", a.shape, mybir.dt.from_np(a.dtype), kind="ExternalInput").ap())
    args.append(nc.dram_tensor("out", (P, C, T), mybir.dt.float32, kind="ExternalOutput").ap())
    build(nc, *args)
    result = run_bass_kernel_spmd(nc, [arrays], core_ids=[0]).results[0]["out"]
    return result.transpose(2, 1, 0).reshape(1, T, D)
```

```python
import math
from contextlib import ExitStack

import numpy as np

import concourse.bass as bass
from concourse import mybir

P = 128
T = 256
TT = T // P
D = 1024
C = D // P
F1 = 4 * D
F2 = ((8 * D // 3 + 255) // 256) * 256
NH = 4
QK = D // (2 * NH)
VD = D // NH
RW = D // 2
RH = RW // NH
XH = D // NH
WINDOWS = (2, 4, 8, 16)
EPS = 1e-6
CAP = 15.0
ROPE_BASE = 10000.0
BLOCKED = -1.0e30

SLAB = 16 * P
HALF = SLAB // 2
RAW = 4
HL = 2

PHASES = [
    ("qk", 4, 4, "V"), ("v", 4, 4, "A"), ("o", 4, 4, "V"),
    ("out0", 4, 4, "A"), ("f4", 1, 1, "A"), ("f0", 1, 1, "V"), ("up0", 16, 16, "V"), ("down0", 16, 4, "A"), ("f1", 1, 1, "V"),
    ("cin", 12, 12, "AVV"), ("out1", 4, 4, "A"), ("f5", 1, 1, "A"), ("f2", 1, 1, "V"),
    ("up1", 16, 16, "V"), ("down1", 16, 4, "A"), ("f6", 1, 1, "A"), ("f3", 1, 1, "V"),
    ("rq", 4, 4, "V"), ("ru", 2, 2, "V"), ("rv", 2, 2, "A"), ("rg", 2, 2, "V"), ("out2", 4, 4, "V"),
    ("wq", 4, 4, "V"), ("f7", 1, 1, "A"), ("wo", 4, 4, "V"),
    ("fup", 2 * F2 // 256, 2 * F2 // 256, "V"), ("fdown", F2 // P // 2, 4, "V"),
]
SLAB0, GROUP0, DRAIN = {}, {}, []
_s = _g = 0
_count = {"A": 0, "V": 0}
for _name, _ns, _ng, _eng in PHASES:
    SLAB0[_name], GROUP0[_name] = _s, _g
    for _i in range(_ng):
        _e = _eng[_i % len(_eng)]
        _count[_e] += 1
        DRAIN.append((_e, _count[_e]))
    _s, _g = _s + _ns, _g + _ng
SLABS = _s

PCOL, _c = {}, 0
for _name, _n in [("g00", C), ("g01", C), ("g02", C), ("g03", C), ("g10", C), ("g11", C), ("g12", C), ("g13", C),
                  ("ghn", C), ("wconv", 3 * C), ("gmix", C), ("gret", NH), ("pscale", NH), ("gxa", C), ("gmem", C),
                  ("gffn", C), ("fw", 3 * 2 * F2 // P), ("fb", 2 * F2 // P), ("gfin", C), ("bgates", 2 * NH)]:
    PCOL[_name] = _c
    _c += _n
NPAR = _c
FT = 2 * F2 // P
FC = F2 // P

NORMS = ["pre", "pre", "post", "pre", "post", "pre", "post", "pre", "post", "pre", "pre", "pre", "last"]


def build(nc, xT, memT, pos, weights, wgate, params, poolw, tri, mask, select, decay, freq, recount, out):
    f32, f32r, i32 = mybir.dt.float32, mybir.dt.float32r, mybir.dt.int32
    ALU, ACT, AX = mybir.AluOpType, mybir.ActivationFunctionType, mybir.AxisListType

    ctx = ExitStack()
    with ctx:
        place = [nc.sbuf_base + (-nc.sbuf_base) % 64]

        def sb(name, shape, dt, at=None):
            size = int(np.prod(shape[1:])) * 4
            if at is None:
                off = place[0]
                place[0] += (size + 31) // 32 * 32
            else:
                off = at[0]
                at[0] += (size + 31) // 32 * 32
            return nc.alloc_sbuf_tensor_at(name, list(shape), dt, offset=off)

        def sem(name):
            return ctx.enter_context(nc.semaphore(name))

        raw = [sb(f"raw{i}", [P, SLAB], f32) for i in range(RAW)]
        wH = [sb(f"wH{i}", [P, SLAB], f32r) for i in range(HL)]
        wL = [sb(f"wL{i}", [P, SLAB], f32r) for i in range(HL)]
        x = sb("x", [P, C, T], f32)
        xnH = sb("xnH", [P, C, T], f32r)
        xnL = sb("xnL", [P, C, T], f32r)
        memH = sb("memH", [P, C, T], f32r)
        memL = sb("memL", [P, C, T], f32r)
        memk = sb("memk", [P, C, T], f32)
        memv = sb("memv", [P, TT, D], f32)
        ident = sb("ident", [P, P], f32)
        ones = sb("ones", [P, P], f32)
        par = sb("par", [P, NPAR], f32)
        Rs = sb("Rs", [P, T], f32)
        Rm = sb("Rm", [P, T], f32)
        diag = sb("diag", [P, TT, P], f32)
        warm = sb("warm", [P, 1], f32)
        ms = sb("ms", [P, TT], f32)
        minus_half = sb("minus_half", [P, 2 * NH], f32)
        rtok = sb("rtok", [P, TT], f32)
        rmem = sb("rmem", [P, TT], f32)
        scratch = place[0]
        at = [scratch]
        y = sb("y", [P, C, T], f32, at)
        squares = sb("squares", [P, 4, 2, T], f32, at)
        sq = [squares[:, i, :, :] for i in range(4)]
        end = at[0]
        at = [scratch]
        hrelu = [sb(f"hrelu{i}", [P, 2, T], f32, at) for i in range(2)]
        hsq = [sb(f"hsq{i}", [P, 2, T], f32, at) for i in range(2)]
        at = [scratch + C * T * 4]
        ang = sb("ang", [P, T], f32, at)
        turn = sb("turn", [P, T], f32, at)
        part = sb("part", [P, T], f32, at)
        at = [scratch]
        mem = sb("mem", [P, C, T], f32, at)
        at = [scratch]
        apad = [sb(f"apad{i}", [P, 2, T + 2], f32, at) for i in range(2)]
        cgate = sb("cgate", [P, 2, T], f32, at)
        cval = sb("cval", [P, 2, T], f32, at)
        assert at[0] <= scratch + C * T * 4 + 64
        place[0] = end
        region = place[0]
        at = [region]
        hH = sb("hH", [P, F1 // P, T], f32r, at)
        hL = sb("hL", [P, F1 // P, T], f32r, at)
        hidden_end = at[0]
        cost = sb("cost", [P, T], f32, at)
        posi = sb("posi", [P, T], i32, [at[0]])
        sint = sb("sint", [P, T], f32, at)
        freqt = sb("freqt", [P, 1], f32, at)
        place[0] = at[0]

        at = [region]
        mixH = sb("mixH", [P, C, T], f32r, at)
        mixL = sb("mixL", [P, C, T], f32r, at)
        mixer = at[0]
        used = [at[0]]
        qT = sb("qT", [P, NH, T], f32, at)
        kT = sb("kT", [P, NH, T], f32, at)
        vx = sb("vx", [P, TT, NH, VD + 1], f32, at)
        sigo = sb("sigo", [P, C, T], f32, at)
        trit = sb("trit", [P, P], f32, at)
        maskt = sb("maskt", [P, T], f32, at)
        selt = sb("selt", [NH, NH, P], f32, at)
        used2 = [at[0]]
        dargs = sb("dargs", [P, T + P], f32, at)
        dexp = sb("dexp", [P, T + P], f32, at)
        prob = [sb(f"prob{h}", [P, T + P], f32, at) for h in range(NH)]
        num = [sb(f"num{i}", [P, TT, VD + 1], f32, used) for i in range(2)]
        hn = [sb(f"hn{i}", [P, TT, VD], f32, w) for i, w in enumerate((used, at))]
        junk = sb("junk", [P, VD], f32, at)
        mixf = sb("mixf", [P, 2, T], f32, used2)
        wg = sb("wg", [P, C, 2 * NH], f32, at)
        wgs = sb("wgs", [P, C, 2 * NH], f32, at)
        gz = sb("gz", [P, TT, 2 * NH], f32, at)
        gt = sb("gt", [P, TT, 2 * NH], f32, at)
        gcap = sb("gcap", [P, TT, 2 * NH], f32, at)
        fexp = sb("fexp", [P, TT, NH], f32, at)
        softp = sb("softp", [P, TT, NH], f32, at)
        nb = sb("nb", [P, TT, NH], f32, at)
        av = sb("av", [P, TT, NH], f32, at)
        mrow = [sb(f"mrow{i}", [NH, P + T], f32, at) for i in range(2)]
        mdiff = sb("mdiff", [P, TT, NH], f32, at)
        em = sb("em", [P, TT, NH], f32, at)
        ssq = sb("ssq", [P, NH, TT], f32, at)
        den = sb("den", [P, NH, TT], f32, at)
        rec = sb("rec", [P, NH, TT], f32, at)
        rec2 = sb("rec2", [P, NH, TT], f32, at)
        hms = sb("hms", [P, NH, TT], f32, at)
        hr = sb("hr", [P, NH, TT], f32, at)
        hc = sb("hc", [P, NH, TT], f32, at)
        assert at[0] <= place[0], at
        at = [mixer]
        csb = sb("csb", [P, 2, T], f32, at)
        cx = sb("cx", [P, 2, T], f32, at)
        upad = sb("upad", [P, 2, T + 2], f32, at)
        conv = sb("conv", [P, 2, T], f32, at)
        bsb = sb("bsb", [P, 2, T], f32, at)
        cout = sb("cout", [P, 2, T], f32, at)
        R2 = sb("R2", [P, T], f32, at)
        at = [mixer]
        rq = sb("rq", [P, NH, T], f32, at)
        rk = sb("rk", [P, NH, T], f32, at)
        rv = sb("rv", [P, TT, RW], f32, at)
        rsg = sb("rsg", [P, NH, T], f32, at)
        rot = sb("rot", [P, 2, T], f32, at)
        ropc = sb("ropc", [P, 2, T], f32, at)
        rops = sb("rops", [P, 2, T], f32, at)
        decayt = sb("decayt", [P, NH, T], f32, at)
        ro = sb("ro", [P, NH, T], f32, at)
        rosq = sb("rosq", [P, NH, T], f32, at)
        at2 = [at[0]]
        rms8 = sb("rms8", [P, NH, TT], f32, at2)
        rr8 = sb("rr8", [P, NH, TT], f32, at2)
        poolwt = sb("poolwt", [P, NH, P], f32, at2)
        recountt = sb("recountt", [P, NH, 16], f32, at2)
        PADW = 16
        upl = [sb(f"upl{i}", [P, 2, PADW + T], f32, at2) for i in range(2)]
        sl = [sb(f"sl{i}", [P, PADW + T], f32, at2) for i in range(2)]
        assert at2[0] <= hidden_end, at2
        pooled, yret = ropc, rops
        ret_y = (yret, pooled)
        at = [scratch]
        rs = [sb(f"rs{i}", [P, T + P], f32, at) for i in range(NH)]
        rdiag = [sb(f"rdiag{i}", [P, TT, P], f32, at) for i in range(2)]
        assert at[0] <= scratch + C * T * 4
        at = [mixer]
        xq = [sb(f"xq{i}", [P, 2, T], f32, at) for i in range(2)]
        xp = [sb(f"xp{i}", [P, TT, T], f32, at) for i in range(2)]
        xpn = [sb(f"xpn{i}", [P, TT, T], f32, at) for i in range(2)]
        xpT = [sb(f"xpT{i}", [P, TT, T], f32, at) for i in range(2)]
        xmax = sb("xmax", [P, NH, TT], f32, at)
        xneg = sb("xneg", [P, NH, TT], f32, at)
        xsum = sb("xsum", [P, NH, TT], f32, at)
        xrec = sb("xrec", [P, NH, TT], f32, at)
        assert place[0] <= nc.sbuf_usable_end, (place, nc.sbuf_usable_end)

        po = [ctx.enter_context(nc.psum_tensor(f"po{i}", [P, 2, 512], f32)) for i in range(2)]
        pn = ctx.enter_context(nc.psum_tensor("pn", [P, 512], f32))
        pa = ctx.enter_context(nc.psum_tensor("pa", [P, 512], f32))
        pb = ctx.enter_context(nc.psum_tensor("pb", [P, 512], f32))
        pc = ctx.enter_context(nc.psum_tensor("pc", [P, 512], f32))

        bank_of = (pb, pc, pn, pa)

        s_raw = [sem(f"raw_loaded{i}") for i in range(RAW)]
        s_hi, s_lo = sem("weights_hi"), sem("weights_lo")
        s_slab = sem("slab_done")
        s_half = sem("first_half_done")
        s_first = sem("first_half_loaded")
        s_group = sem("glu_group_done")
        s_drain = {"A": sem("drained_act"), "V": sem("drained_dve")}
        s_par, s_cst, s_mem = sem("params_loaded"), sem("ident_and_wgates_loaded"), sem("memory_loaded")
        s_x = [sem(f"x_loaded{i}") for i in range(4)]
        s_set, s_causal = sem("constants_set"), sem("masks_loaded")
        s_xnH, s_xn = sem("xn_hi"), sem("xn_ready")
        s_mmH, s_mm = sem("memory_hi"), sem("memory_ready")
        s_sq, s_sqa = sem("squares"), sem("squares_added")
        s_sum, s_ms, s_r, s_diag, s_R = sem("sumsq"), sem("mean_sq"), sem("r_ready"), sem("diag_ready"), sem("R_done")
        s_Rs = sem("R_kept")
        s_t, s_xadd, s_xaddV = sem("y_scaled"), sem("x_added_pool"), sem("x_added_dve")
        s_dch, s_ach, s_pch = sem("dve_chain"), sem("act_chain"), sem("pool_chain")
        s_mixH, s_mix = sem("mix_hi"), sem("mix_ready")
        s_hs, s_hidH, s_hid = sem("hidden_squared"), sem("hidden_hi"), sem("hidden_ready")
        s_wgs, s_gates, s_gz, s_gt, s_gcap, s_sp = [sem("gates_" + n) for n in (
            "weights_gained", "multiplied", "biased", "tanh", "capped", "softplus")]
        s_cum, s_av, s_avT, s_mrow, s_mT, s_md, s_em = [sem("m_" + n) for n in (
            "log_sums", "a", "a_turned", "row_maxima", "maxima_turned", "minus_m", "exp_minus_m")]
        s_osig = sem("output_gate_sigmoid")
        s_S, s_darg, s_dexp, s_P, s_num, s_numk = [sem("head_" + n) for n in (
            "scores", "exponents", "decays", "probabilities", "numerator", "numerator_kept")]
        s_hms, s_hr, s_hn, s_hT, s_mixf = [sem("head_" + n) for n in ("mean_sq", "r", "normed", "turned", "gated")]
        s_u, s_cv, s_cf = [sem("conv_" + n) for n in ("input", "last_tap", "output")]
        s_pos, s_rc = sem("positions_loaded"), sem("retention_consts_loaded")
        s_trig, s_trigd = sem("angles_ready"), sem("sine_cosine")
        s_rot, s_ropc, s_rops, s_rqk = [sem("rotary_" + n) for n in ("halves_swapped", "cosine_part", "sine_part", "done")]
        s_rS, s_rs, s_rO, s_ro = [sem("ret_" + n) for n in ("scores", "decayed", "output", "output_kept")]
        s_rsum, s_rms, s_rr, s_rdiag, s_rR, s_rscaled, s_rsg, s_ry = [sem("ret_" + n) for n in (
            "sumsq", "mean_sq", "r", "diag", "R", "scaled", "gate_silu", "gated")]
        s_pool, s_pw, s_pf = [sem("pool_" + n) for n in ("means", "multiplied", "scaled")]
        s_xs, s_xneg, s_xe, s_xpn, s_xT, s_xpT, s_xo = [sem("xa_" + n) for n in (
            "scores", "minus_max", "exp", "normed", "turned", "turned_kept", "output")]
        s_fc, s_fcd, s_fs, s_fh, s_fH, s_f = [sem("glu_" + n) for n in (
            "last_tap", "other_taps", "silu", "product", "hi", "ready")]
        s_gained = sem("output_gained")
        s_outv, s_outp, s_out = sem("output_ready_dve"), sem("output_ready_pool"), sem("output_stored")

        def col(name, i=0, n=1):
            return par[:, PCOL[name] + i:PCOL[name] + i + n]

        def over_pair(ap):
            return ap.rearrange("p (a t) -> p a t", a=1).to_broadcast([P, 2, T])

        def slot(g):
            return po[g % 2]

        def kept_before(norm):
            pre = sum(k == "pre" for k in NORMS[:norm])
            return pre, norm - pre

        def squares_added(norm):
            pre, other = kept_before(norm)
            return 5 * pre + 3 * other

        def group_done(p):
            ends = [(2 * FC * (q + 1) - 1) % 16 for q in range(p + 1)]
            s = SLAB0["fdown"] + (2 * FC * (p + 1) - 1) // 16
            if ends[p] == 15:
                return s_slab, s + 1
            if ends[p] == 7:
                return s_half, s + 1
            return s_group, sum(e % 8 != 7 for e in ends)

        block = ctx.enter_context(nc.Block())

        @block.sync
        def _(sp):
            sp.dma_start(x[:, 0:2, :], xT[:, 0:2, :]).then_inc(s_x[0], 16)
            sp.dma_start(par[:, :], params).then_inc(s_par, 16)
            sp.dma_start(raw[0][:, 0:HALF], weights[0, :, 0:HALF]).then_inc(s_first, 16)
            sp.dma_start(x[:, 2:4, :], xT[:, 2:4, :]).then_inc(s_x[1], 16)
            sp.dma_start(raw[0][:, HALF:], weights[0, :, HALF:]).then_inc(s_raw[0], 16)
            for p in range(2, 4):
                sp.dma_start(x[:, 2 * p:2 * p + 2, :], xT[:, 2 * p:2 * p + 2, :]).then_inc(s_x[p], 16)
            sp.dma_start(raw[1][:, :], weights[1, :, :]).then_inc(s_raw[1], 16)
            for dst, src in [(ident[:, :], tri[1, :, :]), (wg[:, :, :], wgate)]:
                sp.dma_start(dst, src).then_inc(s_cst, 16)
            sp.dma_start(raw[2][:, :], weights[2, :, :]).then_inc(s_raw[2], 16)
            for dst, src in [(trit[:, :], tri[0, :, :]), (maskt[:, :], mask), (selt[:, :, :], select)]:
                sp.dma_start(dst, src).then_inc(s_causal, 16)
            sp.dma_start(raw[3][:, :], weights[3, :, :]).then_inc(s_raw[3], 16)
            sp.dma_start(mem[:, :, :], memT).then_inc(s_mem, 16)
            for dst, src in [(posi[:, :], pos.partition_broadcast(P)), (freqt[:, :], freq)]:
                sp.dma_start(dst, src).then_inc(s_pos, 16)

            def load(s, slot_):
                sp.wait_ge(s_lo, s * 2 - 6)
                sp.dma_start(raw[slot_][:, :], weights[s, :, :]).then_inc(s_raw[slot_], 16)

            stop = SLAB0["rq"] // RAW + 1
            with sp.Fori(1, stop) as i:
                for j in range(RAW):
                    load(i * RAW + j, j)
            sp.wait_ge(s_slab, SLAB0["f6"])
            for dst, src in [(decayt[:, :, :], decay), (poolwt[:, :, :], poolw), (recountt[:, :, :], recount)]:
                sp.dma_start(dst, src).then_inc(s_rc, 16)
            with sp.Fori(stop, SLABS // RAW) as i:
                for j in range(RAW):
                    load(i * RAW + j, j)
            for s in range(SLABS // RAW * RAW, SLABS):
                load(s, s % RAW)
            for p in range(4):
                if p < 3:
                    sp.wait_ge(s_outv, p + 1)
                else:
                    sp.wait_ge(s_outp, 1)
                sp.dma_start(out[:, 2 * p:2 * p + 2, :], y[:, 2 * p:2 * p + 2, :]).then_inc(s_out, 16)
            sp.wait_ge(s_out, 64)

        @block.tensor
        def _(pe):
            def weights_ready(s, half):
                pe.wait_ge(s_lo, s * 2 + half + 1)

            def slot_free(g):
                if g >= 2:
                    e, n = DRAIN[g - 2]
                    pe.wait_ge(s_drain[e], n)

            def products(psum, n, w, k, aH, aL, ac, start, stop):
                wc = slice(k * 256 + n * P, k * 256 + (n + 1) * P)
                pe.matmul(psum[:, n, 0:T], wH[w][:, wc], aH[:, ac, :], start=start, stop=False)
                pe.matmul(psum[:, n, 0:T], wH[w][:, wc], aL[:, ac, :], start=False, stop=False)
                return pe.matmul(psum[:, n, 0:T], wL[w][:, wc], aH[:, ac, :], start=False, stop=stop)

            def slab(s, w, psum, aH, aL, c0=0, first=True, last=True, ready=None, between={}):
                for k in range(8):
                    if k % 4 == 0:
                        weights_ready(s, k // 4)
                    if ready and k % 2 == 0:
                        pe.wait_ge(ready[0], ready[1] + k // 2 + 1)
                    for n in range(2):
                        mm = products(psum, n, w, k, aH, aL, c0 + k, first and k == 0, last and k == 7)
                    if k == 3:
                        mm.then_inc(s_half, 1)
                    if k in between:
                        between[k]()
                mm.then_inc(s_slab, 1)

            def slab_by_token(s, w, psum, aH, aL, between={}):
                for k in range(8):
                    if k % 4 == 0:
                        weights_ready(s, k // 4)
                    wc = slice(k * 256, k * 256 + 256)
                    for t in range(TT):
                        tc = slice(t * P, t * P + P)
                        pe.matmul(psum[:, t, 0:256], aH[:, k, tc], wH[w][:, wc], start=k == 0, stop=False)
                        pe.matmul(psum[:, t, 0:256], aL[:, k, tc], wH[w][:, wc], start=False, stop=False)
                        mm = pe.matmul(psum[:, t, 0:256], aH[:, k, tc], wL[w][:, wc], start=False, stop=k == 7)
                    if k == 3:
                        mm.then_inc(s_half, 1)
                    if k in between:
                        between[k]()
                mm.then_inc(s_slab, 1)

            def phase_slab(name, i, aH, aL, by_token=False, ready=None, between={}):
                s, g = SLAB0[name] + i, GROUP0[name] + i
                slot_free(g)
                if by_token:
                    slab_by_token(s, s % HL, slot(g), aH, aL, between)
                else:
                    slab(s, s % HL, slot(g), aH, aL, ready=ready, between=between)

            def fill(n, between={}):
                if n == 4:
                    pe.wait_ge(s_mm, 4)
                phase_slab(f"f{n}", 0, memH, memL, by_token=n >= 4, between=between)

            def norm_sums(n):
                if n:
                    pre, other = kept_before(n)
                    if NORMS[n - 1] == "pre":
                        pe.wait_ge(s_Rs, pre)
                    else:
                        pe.wait_ge(s_t, 4 * other)
                if n == 1:
                    pe.wait_ge(s_darg, NH)
                pe.wait_ge(s_sqa, squares_added(n + 1))
                pe.wait_ge(s_sq, 4 * n + 4)
                for t in range(TT):
                    tc = slice(t * P, t * P + P)
                    squared = [sq[0][:, 0, tc]]
                    if NORMS[n] != "pre":
                        squared += [sq[3][:, 0, tc], sq[3][:, 1, tc]]
                    for k, chunk in enumerate(squared):
                        mm = pe.matmul(pn[:, t:t + 1], chunk, ones[:, 0:1], start=k == 0, stop=k == len(squared) - 1)
                mm.then_inc(s_sum, 1)

            def norm_spread(n):
                pe.wait_ge(s_diag, n + 1)
                for t in range(TT):
                    mm = pe.matmul(pn[:, 128 + t * P:128 + (t + 1) * P], ones[:, :], diag[:, t, :], start=True, stop=True)
                mm.then_inc(s_R, 1)

            def norm(n):
                return {2: lambda: norm_sums(n), 5: lambda: norm_spread(n)}

            def scores(h):
                bank, row = (pc, pn) if h % 2 else (pa, pb)
                if h == 1:
                    pe.wait_ge(s_md, 1)
                if h >= 2:
                    pe.wait_ge(s_P, h - 1)
                    pe.wait_ge(s_darg, h - 1)
                pe.matmul(bank[:, 0:T], kT[:, h, 0:P], qT[:, h, :], start=True, stop=True)
                pe.matmul(bank[:, T:T + P], kT[:, h, P:T], qT[:, h, P:T], start=True, stop=True)
                pe.matmul(row[:, 0:T], selt[:, h, :], mrow[0][:, P:P + T], start=True, stop=True).then_inc(s_S, 1)

            def numerator(h):
                pe.wait_ge(s_P, NH)
                pe.wait_ge(s_drain["A"], h + 1)
                if h == 0:
                    pe.wait_ge(s_darg, NH)
                else:
                    pe.wait_ge(s_numk, h)
                pe.matmul(pc[:, 0:VD + 1], prob[h][:, 0:P], vx[:, 0, h, :], start=True, stop=True)
                pe.matmul(pb[:, 0:VD + 1], prob[h][:, P:T], vx[:, 0, h, :], start=True, stop=False)
                pe.matmul(pb[:, 0:VD + 1], prob[h][:, T:T + P], vx[:, 1, h, :], start=False, stop=True)\
                    .then_inc(s_num, 1)

            def turn_head(h):
                pe.wait_ge(s_hn, h + 1)
                if h == 0:
                    pe.wait_ge(s_Rs, 2)
                else:
                    pe.wait_ge(s_mixf, h)
                for e in range(2):
                    for t in range(TT):
                        mm = pe.transpose(pn[:, e * T + t * P:e * T + t * P + P],
                                          hn[h % 2][:, t, e * P:(e + 1) * P], ident[:, :])
                mm.then_inc(s_hT, 1)

            def gates(t, chunks):
                pe.wait_ge(s_wgs, 1)
                for k in chunks:
                    mm = pe.matmul(pa[:, t * 8:t * 8 + 8], x[:, k, t * P:(t + 1) * P], wgs[:, k, :], start=k == 0, stop=k == C - 1)
                if t == TT - 1 and k == C - 1:
                    mm.then_inc(s_gates, 1)

            def log_sums():
                pe.wait_ge(s_causal, 48)
                pe.wait_ge(s_sp, 1)
                pe.wait_ge(s_gz, 1)
                pe.matmul(pa[:, 0:NH], trit[:, :], softp[:, 0, :], start=True, stop=True)
                pe.matmul(pa[:, NH:2 * NH], trit[:, :], softp[:, 1, :], start=True, stop=False)
                pe.matmul(pa[:, NH:2 * NH], ones[:, :], softp[:, 0, :], start=False, stop=True).then_inc(s_cum, 1)

            def turn_a():
                pe.wait_ge(s_av, 1)
                for t in range(TT):
                    mm = pe.transpose(pb[0:NH, t * P:(t + 1) * P], av[:, t, :], ident[:, :])
                mm.then_inc(s_avT, 1)

            def turn_maxima():
                pe.wait_ge(s_mrow, 1)
                pe.wait_ge(s_Rs, 1)
                for t in range(TT):
                    mm = pe.transpose(pn[:, t * NH:(t + 1) * NH], mrow[0][:, P + t * P:P + (t + 1) * P], ident[0:NH, 0:NH])
                mm.then_inc(s_mT, 1)

            def first_scores():
                pe.wait_ge(s_drain["V"], 4)
                pe.wait_ge(s_mrow, 1)
                scores(0)

            pe.wait_ge(s_set, 1)
            for _ in range(14):
                pe.matmul(pn[:, 0:P], ones[:, :], ones[:, :], start=True, stop=True)
            phase_slab("qk", 0, xnH, xnL, ready=(s_xn, 0))
            phase_slab("qk", 1, xnH, xnL, between=norm(0) | {6: lambda: gates(0, range(4)), 7: lambda: gates(0, range(4, 8))})
            phase_slab("qk", 2, xnH, xnL, between={0: lambda: gates(1, range(4)), 1: lambda: gates(1, range(4, 8))})
            phase_slab("qk", 3, xnH, xnL, between={6: log_sums})
            phase_slab("v", 0, xnH, xnL, by_token=True, between={1: turn_a})
            phase_slab("v", 1, xnH, xnL, by_token=True, between={2: first_scores, 3: turn_maxima, 7: lambda: scores(1)})
            phase_slab("v", 2, xnH, xnL, by_token=True, between={4: lambda: scores(2)})
            phase_slab("v", 3, xnH, xnL, by_token=True, between={1: lambda: scores(3)})
            phase_slab("o", 0, xnH, xnL, between={0: lambda: numerator(0), 1: lambda: norm_sums(1), 5: lambda: norm_spread(1),
                                                  6: lambda: numerator(1)})
            phase_slab("o", 1, xnH, xnL, between={1: lambda: turn_head(0), 2: lambda: numerator(2), 6: lambda: turn_head(1),
                                                  7: lambda: numerator(3)})
            phase_slab("o", 2, xnH, xnL, between={5: lambda: turn_head(2)})
            phase_slab("o", 3, xnH, xnL, between={7: lambda: turn_head(3)})

            def fillers(names, n_norm):
                fill(names[0], {1: lambda: norm_sums(n_norm), 4: lambda: norm_spread(n_norm)})
                for n in names[1:]:
                    fill(n)

            def out_phase(name, mix0, names, n_norm, between={}):
                for i in range(4):
                    phase_slab(name, i, mixH, mixL, ready=(s_mix, mix0) if i == 0 else None, between=between if i == 0 else {})
                fillers(names, n_norm)

            def mlp(layer, feed, n_norm, names):
                up, down = f"up{layer}", f"down{layer}"
                s0, g0 = SLAB0[up], GROUP0[up]
                d0 = DRAIN[g0][1]
                for j in range(4):
                    phase_slab(up, j, xnH, xnL, ready=(s_xn, 4 * feed) if j == 0 else None,
                               between=norm(n_norm) if j == 1 else {})
                with pe.Fori(0, 3) as i:
                    for j in range(4):
                        pe.wait_ge(s_drain["V"], i * 4 + (d0 + 4 + j - 2))
                        slab(i * 4 + (s0 + 4 + j), (s0 + j) % HL, slot(g0 + j), xnH, xnL)
                s0, g0 = SLAB0[down], GROUP0[down]
                d0 = DRAIN[g0][1]
                with pe.Fori(0, 2) as i:
                    for j in range(2):
                        slot_free(g0 + j)
                        pe.wait_ge(s_drain["A"], i * 2 + (d0 + j - 2))
                        for kk in range(4):
                            b = s0 + 4 * j + kk
                            slab(i * 8 + b, b % HL, slot(g0 + j), hH, hL, c0=8 * kk, first=kk == 0, last=kk == 3,
                                 ready=(s_hid, 16 * layer + 4 * kk) if j == 0 else None)
                fillers(names, n_norm + 1)

            out_phase("out0", 0, (4, 0), 2)
            mlp(0, 1, 3, (1,))

            for i in range(12):
                phase_slab("cin", i, xnH, xnL, ready=(s_xn, 8) if i == 0 else None, between=norm(5) if i == 1 else {})
            out_phase("out1", 4, (5, 2), 6)
            mlp(1, 3, 7, (6, 3))

            def ret_scores(h):
                pe.wait_ge(s_rqk, 4)
                if h >= 2:
                    pe.wait_ge(s_rs, h - 1)
                bank = pc if h % 2 else pa
                pe.matmul(bank[:, 0:T], rk[:, h, 0:P], rq[:, h, :], start=True, stop=True)
                pe.matmul(bank[:, T:T + P], rk[:, h, P:T], rq[:, h, P:T], start=True, stop=True).then_inc(s_rS, 1)

            def ret_values(h):
                pe.wait_ge(s_rs, h + 1)
                pe.wait_ge(s_drain["A"], DRAIN[GROUP0["rv"] + 1][1])
                if h == 1:
                    pe.wait_ge(s_rs, NH)
                if h == 2:
                    pe.wait_ge(s_Rs, kept_before(10)[0])
                if h == 3:
                    pe.wait_ge(s_pf, 1)
                bank = bank_of[h]
                pe.matmul(bank[:, 0:T], rv[:, 0, h * RH:(h + 1) * RH], rs[h][:, 0:T], start=True, stop=False)
                pe.matmul(bank[:, P:T], rv[:, 1, h * RH:(h + 1) * RH], rs[h][:, T:T + P], start=False, stop=True)\
                    .then_inc(s_rO, 1)

            def pool_product(j):
                pe.wait_ge(s_pool, j + 1)
                pe.wait_ge(s_rc, 48)
                if j:
                    pe.wait_ge(s_ro, 1)
                else:
                    pe.wait_ge(s_rs, 3)
                for e in range(2):
                    mm = pe.matmul((pb if j else pa)[:, e * T:(e + 1) * T], poolwt[:, 2 * j + e, :], pooled[:, e, :], start=True, stop=True)
                mm.then_inc(s_pw, 1)

            def head_squares():
                pe.wait_ge(s_ro, NH)
                for h in range(NH):
                    for t in range(TT):
                        mm = pe.matmul(pn[:, h * TT + t:h * TT + t + 1], rosq[:, h, t * P:(t + 1) * P], ones[:, 0:1],
                                       start=True, stop=True)
                mm.then_inc(s_rsum, 1)

            def head_spread(h):
                pe.wait_ge(s_rdiag, h + 1)
                bank, c = pc if h >= 2 else pa, h % 2 * T
                for t in range(TT):
                    mm = pe.matmul(bank[:, c + t * P:c + (t + 1) * P], ones[:, :], rdiag[h % 2][:, t, :], start=True, stop=True)
                mm.then_inc(s_rR, 1)

            for i in range(4):
                phase_slab("rq", i, xnH, xnL, ready=(s_xn, 16) if i == 0 else None, between=norm(9) if i == 1 else {})
            phase_slab("ru", 0, xnH, xnL)
            phase_slab("ru", 1, xnH, xnL, between={4: lambda: ret_scores(0), 6: lambda: ret_scores(1)})
            phase_slab("rv", 0, xnH, xnL, by_token=True, between={1: lambda: ret_scores(2), 4: lambda: ret_scores(3)})
            phase_slab("rv", 1, xnH, xnL, by_token=True, between={5: lambda: pool_product(0)})
            phase_slab("rg", 0, xnH, xnL, between={2: lambda: ret_values(0), 3: lambda: ret_values(1), 4: lambda: ret_values(2),
                                                   5: lambda: ret_values(3)})
            phase_slab("rg", 1, xnH, xnL, between={0: lambda: pool_product(1), 1: head_squares, 5: lambda: head_spread(0),
                                                   6: lambda: (head_spread(1), head_spread(2)), 7: lambda: head_spread(3)})
            for i in range(4):
                phase_slab("out2", i, mixH, mixL, ready=(s_mix, 8) if i == 0 else None)

            def xa_scores(h):
                pe.wait_ge(s_drain["V"], DRAIN[GROUP0["wq"] + h][1])
                bank = pn if h % 2 else pa
                if h == 0:
                    pe.wait_ge(s_drain["V"], DRAIN[GROUP0["f3"]][1])
                elif h == 1:
                    pe.wait_ge(s_Rs, kept_before(10)[0] + 1)
                else:
                    pe.wait_ge(s_xe, h - 1)
                for t in range(TT):
                    for c in range(2):
                        mm = pe.matmul(bank[:, t * T:(t + 1) * T], xq[h % 2][:, c, t * P:(t + 1) * P], memk[:, 2 * h + c, :],
                                       start=c == 0, stop=c == 1)
                mm.then_inc(s_xs, 1)

            def xa_turn(h):
                pe.wait_ge(s_xpn, h + 1)
                if h:
                    pe.wait_ge(s_xpT, h)
                for m in range(TT):
                    for t in range(TT):
                        mm = pe.transpose(pb[:, m * T + t * P:m * T + (t + 1) * P], xpn[h % 2][:, t, m * P:(m + 1) * P],
                                          ident[:, :])
                mm.then_inc(s_xT, 1)

            def xa_values(h):
                pe.wait_ge(s_xpT, h + 1)
                pe.wait_ge(s_drain["A"], DRAIN[GROUP0["f7" if h == 3 else "f6"]][1])
                if h:
                    pe.wait_ge(s_mix, 12 + h)
                for c in range(2):
                    for m in range(TT):
                        mm = pe.matmul(pc[:, c * T:(c + 1) * T], memv[:, m, h * XH + c * P:h * XH + (c + 1) * P],
                                       xpT[h % 2][:, m, :], start=m == 0, stop=m == 1)
                mm.then_inc(s_xo, 1)

            phase_slab("wq", 0, xnH, xnL, ready=(s_xn, 20))
            phase_slab("wq", 1, xnH, xnL, between=norm(10))
            phase_slab("wq", 2, xnH, xnL, between={0: lambda: xa_scores(0), 2: lambda: xa_scores(1)})
            phase_slab("wq", 3, xnH, xnL, between={1: lambda: xa_turn(0), 3: lambda: xa_scores(2), 4: lambda: xa_values(0),
                                                   6: lambda: xa_turn(1)})
            fill(7, {1: lambda: xa_scores(3), 2: lambda: xa_values(1), 4: lambda: xa_turn(2), 6: lambda: xa_values(2)})
            for i in range(4):
                phase_slab("wo", i, mixH, mixL, ready=(s_mix, 12) if i == 0 else None,
                           between={0: lambda: xa_turn(3), 2: lambda: xa_values(3)} if i == 0 else {})

            s0, g0 = SLAB0["fup"], GROUP0["fup"]
            d0 = DRAIN[g0][1]
            phase_slab("fup", 0, xnH, xnL, ready=(s_xn, 24))
            phase_slab("fup", 1, xnH, xnL, between=norm(11))
            with pe.Fori(0, (FT // 2 - 2) // 4) as i:
                for j in range(4):
                    pe.wait_ge(s_drain["V"], i * 4 + (d0 + j))
                    slab(i * 4 + (s0 + 2 + j), (s0 + j) % HL, slot(g0 + j), xnH, xnL)
            s0, g0 = SLAB0["fdown"], GROUP0["fdown"]
            for g in range(4):
                slot_free(g0 + g)
                for k in range(FC):
                    for n in range(2):
                        tile = (g * FC + k) * 2 + n
                        s, at_ = s0 + tile // 16, tile % 16
                        if at_ % 8 == 0:
                            weights_ready(s, at_ // 8)
                        if g == 0 and k % 2 == 0 and n == 0:
                            pe.wait_ge(s_f, k // 2 + 1)
                        mm = products(slot(g0 + g), n, s % HL, at_ // 2, hH, hL, k, k == 0, k == FC - 1)
                        if at_ == 7:
                            mm.then_inc(s_half, 1)
                        elif at_ == 15:
                            mm.then_inc(s_slab, 1)
                        elif k == FC - 1 and n == 1:
                            mm.then_inc(s_group, 1)
            norm_sums(12)
            norm_spread(12)

        @block.scalar
        def _(act):
            def split(b, i=None, turns=0, halves=(0, 1)):
                if i is None and b >= SLABS:
                    return
                loaded = 16 * (b // RAW + 1)
                for half in halves:
                    if b == 0 and half == 0:
                        act.wait_ge(s_first, 16)
                    else:
                        act.wait_ge(s_raw[b % RAW], loaded if i is None else i * (16 * turns // RAW) + loaded)
                    if b >= HL:
                        act.wait_ge((s_half, s_slab)[half], b - 1 if i is None else i * turns + (b - 1))
                    hs = slice(half * HALF, (half + 1) * HALF)
                    act.activation(wH[b % HL][:, hs], raw[b % RAW][:, hs], ACT.Copy).then_inc(s_hi, 1)

            chain = [0]

            def link(instruction):
                chain[0] += 1
                instruction.then_inc(s_ach, 1)
                act.wait_ge(s_ach, chain[0])

            def feed_hi(p, gain, ready):
                act.wait_ge(*ready)
                for c in (2 * p, 2 * p + 1):
                    act.activation(xnH[:, c, :], x[:, c, :], ACT.Identity, scale=col(gain, c)).then_inc(s_xnH, 1)

            def feed_squares(p):
                act.activation(sq[p], x[:, 2 * p:2 * p + 2, :], ACT.Square).then_inc(s_sq, 1)

            def feed_pair(p, gain, ready):
                feed_hi(p, gain, ready)
                feed_squares(p)

            def mem_pair(p):
                act.wait_ge(s_mem, 16)
                act.wait_ge(s_sum, 1)
                for c in (2 * p, 2 * p + 1):
                    act.activation(memH[:, c, :], mem[:, c, :], ACT.Identity, scale=col("gmem", c)).then_inc(s_mmH, 1)
                act.activation(sq[p], mem[:, 2 * p:2 * p + 2, :], ACT.Square).then_inc(s_sq, 1)

            def keep_R(n, dst):
                act.wait_ge(s_R, n + 1)
                act.activation(dst, pn[:, 128:128 + T], ACT.Copy).then_inc(s_Rs, 1)

            def group(name, i):
                act.wait_ge(s_slab, SLAB0[name] + i + 1)
                return slot(GROUP0[name] + i)

            def keep_values(name, i, dst, r, norm_done):
                psum = group(name, i)
                act.wait_ge(s_r, norm_done)
                for t in range(TT):
                    k = act.activation(dst(t), psum[:, t, 0:256], ACT.Identity, scale=r[:, t:t + 1])
                k.then_inc(s_drain["A"], 1)

            def keep_y(psum, g, gain):
                act.activation(squares[:, g, :, :], psum[:, :, 0:T], ACT.Square).then_inc(s_sq, 1)
                for e in range(2):
                    if isinstance(g, int):
                        dst, by = y[:, 2 * g + e, :], col(gain, 2 * g + e)
                    else:
                        dst, by = y[:, bass.ts(g * 2 + e, 1), :], par[:, bass.ts(g * 2 + (PCOL[gain] + e), 1)]
                    k = act.activation(dst, psum[:, e, 0:T], ACT.Identity, scale=by)
                k.then_inc(s_drain["A"], 1)

            def mix_hi(src, pair, done):
                act.wait_ge(*done)
                act.activation(mixH[:, 2 * pair:2 * pair + 2, :], src, ACT.Copy).then_inc(s_mixH, 1)

            act.wait_ge(s_set, 1)
            act.activation(warm[:, :], ones[:, 0:1], ACT.Square)
            act.wait_ge(s_par, 16)
            feed_pair(0, "g00", (s_x[0], 16))
            split(0, halves=(0,))
            feed_pair(1, "g00", (s_x[1], 16))
            split(0, halves=(1,))
            feed_pair(2, "g00", (s_x[2], 16))
            feed_pair(3, "g00", (s_x[3], 16))
            split(1)
            split(2)
            keep_R(0, Rs[:, :])
            mem_pair(0)
            split(3)
            act.wait_ge(s_gz, 1)
            act.activation(gt[:, :, :], gz[:, :, :], ACT.Tanh, scale=1.0 / CAP).then_inc(s_gt, 1)
            act.wait_ge(s_gcap, 1)
            link(act.activation(fexp[:, :, :], gcap[:, :, NH:2 * NH], ACT.Exp, scale=-1.0))
            act.activation(softp[:, :, :], fexp[:, :, :], ACT.Ln, bias=1.0).then_inc(s_sp, 1)
            split(4)
            mem_pair(1)
            split(5)
            v0 = SLAB0["v"]

            def keep_vx(h):
                keep_values("v", h, lambda t: vx[:, t, h, 0:VD], rtok, 1)

            def decays(h):
                act.wait_ge(s_darg, h + 1)
                act.activation(dexp[:, 0:T], dargs[:, 0:T], ACT.Exp, bias=av[:, 0, h:h + 1])
                act.activation(dexp[:, T:T + P], dargs[:, T:T + P], ACT.Exp, bias=av[:, 1, h:h + 1]).then_inc(s_dexp, 1)

            def gate_o(i):
                act.wait_ge(s_drain["V"], DRAIN[GROUP0["o"] + i][1])
                act.activation(sigo[:, 2 * i:2 * i + 2, :], sigo[:, 2 * i:2 * i + 2, :], ACT.Sigmoid).then_inc(s_osig, 1)

            def keep_numerator(h):
                act.wait_ge(s_num, h + 1)
                if h:
                    act.wait_ge(s_numk, h)
                if h >= 2:
                    act.wait_ge(s_hn, h - 1)
                for t, bank in enumerate((pc, pb)):
                    act.activation(num[h % 2][:, t, :], bank[:, 0:VD + 1], ACT.Copy)
                    k = act.activation(junk[:, :], bank[:, 0:VD], ACT.Square, accum_out=ssq[:, h, t:t + 1])
                    if t == 0:
                        link(k)
                k.then_inc(s_numk, 1)

            keep_vx(0)
            mem_pair(2)
            split(v0 + 2)
            mem_pair(3)
            decays(0)
            keep_vx(1)
            split(v0 + 3)
            decays(1)
            act.wait_ge(s_md, 1)
            act.activation(em[:, :, :], mdiff[:, :, :], ACT.Exp).then_inc(s_em, 1)
            split(v0 + 4)
            keep_vx(2)
            decays(2)
            decays(3)
            split(v0 + 5)
            keep_vx(3)
            keep_numerator(0)
            split(v0 + 6, halves=(0,))
            keep_R(1, Rm[:, :])
            keep_numerator(1)
            split(v0 + 6, halves=(1,))
            gate_o(0)
            keep_numerator(2)
            split(v0 + 7, halves=(0,))
            mix_hi(mixf[:, :, :], 0, (s_mixf, 1))
            keep_numerator(3)
            gate_o(1)
            split(v0 + 7, halves=(1,))
            mix_hi(mixf[:, :, :], 1, (s_mixf, 2))
            split(v0 + 8, halves=(0,))
            gate_o(2)
            split(v0 + 8, halves=(1,))
            mix_hi(mixf[:, :, :], 2, (s_mixf, 3))
            split(v0 + 9, halves=(0,))
            gate_o(3)
            split(v0 + 9, halves=(1,))
            mix_hi(mixf[:, :, :], 3, (s_mixf, 4))

            def out_phase(name, gain):
                for i in range(4):
                    split(SLAB0[name] + i + 2, halves=(0,))
                    keep_y(group(name, i), i, gain)
                    split(SLAB0[name] + i + 2, halves=(1,))

            def boundary(filler, post, gain, value=None):
                nxt = SLAB0[filler] + 2
                if value is not None:
                    split(nxt)
                    fill_values(value)
                    nxt += 1
                for p in range(4):
                    feed_hi(p, gain, (s_xadd if p % 2 else s_xaddV, 2 * post + p // 2 + 1))
                    if p < 2:
                        feed_squares(p)
                split(nxt, halves=(0,))
                feed_squares(2)
                feed_squares(3)
                split(nxt, halves=(1,))

            def fill_values(h):
                keep_values(f"f{4 + h}", 0, lambda t: memv[:, t, h * XH:(h + 1) * XH], rmem, 2)

            def mlp(layer, gain, n_norm):
                up, down = f"up{layer}", f"down{layer}"
                s0 = SLAB0[up]
                d0 = DRAIN[GROUP0[up]][1]

                def square(n, i=None):
                    def at(v, m=4):
                        return v if i is None else i * m + v
                    act.wait_ge(s_drain["V"], at(d0 + n))
                    act.activation(hsq[n % 2][:, :, :], hrelu[n % 2][:, :, :], ACT.Square).then_inc(s_hs, 1)
                    act.wait_ge(s_hs, at(16 * layer + n + 1))
                    dst = hH[:, 2 * n:2 * n + 2, :] if i is None else hH[:, bass.ts(i * 4 + n, 2), :]
                    act.activation(dst, hsq[n % 2][:, :, :], ACT.Copy).then_inc(s_hidH, 1)

                for n in range(4):
                    split(s0 + n + 2)
                    if n == 0:
                        keep_R(n_norm, Rs[:, :])
                    square(n)
                with act.Fori(0, 3) as i:
                    for j in range(4):
                        split(s0 + 4 + j + 2, i, 4)
                        square(4 + j, i)
                if layer == 1:
                    act.wait_ge(s_trig, 1)
                    act.activation(sint[:, :], ang[:, :], ACT.Sin).then_inc(s_trigd, 1)
                    act.activation(cost[:, :], turn[:, :], ACT.Sin).then_inc(s_trigd, 1)
                    act.wait_ge(s_trigd, 2)
                s0 = SLAB0[down]
                with act.Fori(0, 2) as i:
                    for j in range(2):
                        for kk in range(4):
                            b = s0 + 4 * j + kk
                            split(b + 2, i, 8, halves=(0,))
                            if kk == 3:
                                act.wait_ge(s_slab, i * 8 + (b + 1))
                                keep_y(slot(GROUP0[down] + j), i * 2 + j, gain)
                            split(b + 2, i, 8, halves=(1,))

            out_phase("out0", "g01")
            boundary("f4", 0, "g02", 0)
            mlp(0, "g03", 3)
            boundary("f1", 1, "g10")

            c0 = SLAB0["cin"]
            for i in range(12):
                split(c0 + i + 2)
                if i == 0:
                    keep_R(5, Rs[:, :])
                j = i // 3
                if i % 3 == 0:
                    psum = group("cin", i)
                    if j:
                        act.wait_ge(s_drain["V"], DRAIN[GROUP0["cin"] + i - 2][1])
                    act.activation(csb[:, :, :], psum[:, :, 0:T], ACT.Copy).then_inc(s_drain["A"], 1)
                elif i % 3 == 1:
                    act.wait_ge(s_u, j + 1)
                    for e in range(2):
                        k = act.activation(conv[:, e, :], upad[:, e, 2:], ACT.Identity, scale=col("wconv", 2 * C + 2 * j + e))
                    k.then_inc(s_cv, 1)
                else:
                    mix_hi(cout[:, :, :], j, (s_cf, j + 1))
            out_phase("out1", "g11")
            boundary("f5", 2, "g12", 1)
            mlp(1, "g13", 7)
            boundary("f6", 3, "gmix", 2)

            r0 = SLAB0["rq"]
            for i in range(4):
                split(r0 + i + 2)
                if i == 0:
                    keep_R(9, Rs[:, :])
                act.wait_ge(s_drain["V"], DRAIN[GROUP0["rq"] + i][1])
                if i:
                    act.wait_ge(s_rops, i)
                src = (rq if i < 2 else rk)[:, 2 * (i % 2):2 * (i % 2) + 2, :]
                act.activation(rot[0:64, :, :], src[64:128, :, :], ACT.Copy, scale=-1.0)
                act.activation(rot[64:128, :, :], src[0:64, :, :], ACT.Copy).then_inc(s_rot, 1)

            def keep_o(h):
                act.wait_ge(s_rO, h + 1)
                act.activation(ro[:, h, :], bank_of[h][:, 0:T], ACT.Copy)
                act.activation(rosq[:, h, :], bank_of[h][:, 0:T], ACT.Square).then_inc(s_ro, 1)

            def silu_g(i):
                act.wait_ge(s_drain["V"], DRAIN[GROUP0["rg"] + i][1])
                act.activation(rsg[:, 2 * i:2 * i + 2, :], rsg[:, 2 * i:2 * i + 2, :], ACT.Silu).then_inc(s_rsg, 1)

            def pool_out(j):
                act.wait_ge(s_pw, j + 1)
                if j:
                    act.wait_ge(s_mix, 8 + j)
                for e in range(2):
                    k = act.activation(yret[:, e, :], (pb if j else pa)[:, e * T:(e + 1) * T], ACT.Identity, scale=col("pscale", 2 * j + e))
                k.then_inc(s_pf, 1)
                mix_hi(yret[:, :, :], j, (s_pf, j + 1))

            u0 = SLAB0["ru"]
            split(u0 + 2)
            split(u0 + 3)
            for i in range(2):
                split(u0 + i + 4)
                keep_values("rv", i, lambda t: rv[:, t, i * 256:(i + 1) * 256], rtok, 10)
            pool_out(0)
            for h in range(NH):
                keep_o(h)
            split(u0 + 6)
            silu_g(0)
            pool_out(1)
            split(u0 + 7)
            mix_hi(ret_y[0][:, :, :], 2, (s_ry, 1))
            silu_g(1)
            mix_hi(ret_y[1][:, :, :], 3, (s_ry, 2))

            def residual(name):
                return lambda p: (s_drain["V"], DRAIN[GROUP0[name] + p][1])

            for i in range(4):
                split(SLAB0["out2"] + i + 2)
                feed_pair(i, "gxa", residual("out2")(i))

            def softmax(h):
                act.wait_ge(s_xneg, h + 1)
                if h >= 2:
                    act.wait_ge(s_xpn, h - 1)
                bank = pn if h % 2 else pa
                for t in range(TT):
                    k = act.activation(xp[h % 2][:, t, :], bank[:, t * T:(t + 1) * T], ACT.Exp, scale=XH ** -0.5,
                                       bias=xneg[:, h, t:t + 1], accum_out=xsum[:, h, t:t + 1])
                k.then_inc(s_xe, 1)

            def xa_hi(h):
                mix_hi(pc[:, :].rearrange("p (a t) -> p a t", a=2), h, (s_xo, h + 1))

            def keep_turned(h):
                act.wait_ge(s_xT, h + 1)
                if h >= 2:
                    act.wait_ge(s_xo, h - 1)
                act.activation(xpT[h % 2][:, :, :], pb[:, :].rearrange("p (m t) -> p m t", m=TT), ACT.Copy).then_inc(s_xpT, 1)

            q0 = SLAB0["wq"]
            split(q0 + 2)
            keep_R(10, Rs[:, :])
            split(q0 + 3)
            softmax(0)
            softmax(1)
            split(q0 + 4)
            keep_turned(0)
            xa_hi(0)
            softmax(2)
            keep_turned(1)
            split(q0 + 5)
            xa_hi(1)
            softmax(3)
            keep_turned(2)
            split(q0 + 6, halves=(0,))
            xa_hi(2)
            fill_values(3)
            split(q0 + 6, halves=(1,))
            keep_turned(3)
            xa_hi(3)
            for i in range(4):
                split(SLAB0["wo"] + i + 2)
                feed_pair(i, "gffn", residual("wo")(i))

            s0, d0 = SLAB0["fup"], DRAIN[GROUP0["fup"]][1]
            side = [cgate, cval]
            wcol, bcol = PCOL["fw"] + 2 * FT, PCOL["fb"]

            def taps(n, i=None):
                def at(v, m=4):
                    return v if i is None else i * m + v
                act.wait_ge(s_drain["V"], at(d0 + n))
                if n >= 2:
                    if n % 2 == 0:
                        act.wait_ge(s_fh, at(n // 2, 2))
                    else:
                        act.wait_ge(s_f, at(n // 2, 2))
                for e in range(2):
                    t = 2 * n + e
                    if i is None:
                        w, b = par[:, wcol + t:wcol + t + 1], par[:, bcol + t:bcol + t + 1]
                    else:
                        w, b = par[:, bass.ts(i * 8 + (wcol + t), 1)], par[:, bass.ts(i * 8 + (bcol + t), 1)]
                    k = act.activation(side[n % 2][:, e, :], apad[n % 2][:, e, 2:], ACT.Identity, scale=w, bias=b)
                k.then_inc(s_fc, 1)

            def behind(n, i=None):
                def at(v, m=4):
                    return v if i is None else i * m + v
                if n % 2 == 0:
                    act.wait_ge(s_fcd, at(2 * n + 2, 8))
                    act.activation(cgate[:, :, :], cgate[:, :, :], ACT.Silu).then_inc(s_fs, 1)
                else:
                    m = n // 2
                    act.wait_ge(s_fh, at(m + 1, 2))
                    dst = hH[:, 2 * m:2 * m + 2, :] if i is None else hH[:, bass.ts(i * 2 + m, 2), :]
                    act.activation(dst, cval[:, :, :], ACT.Copy).then_inc(s_fH, 1)

            split(s0 + 2)
            keep_R(11, Rs[:, :])
            taps(0)
            split(s0 + 3)
            behind(0)
            taps(1)
            with act.Fori(0, (FT // 2 - 2) // 4) as i:
                for j in range(4):
                    split(s0 + 4 + j, i, 4)
                    behind(1 + j, i)
                    taps(2 + j, i)
            def last_squares(p):
                feed_squares(p)
                for c in (2 * p, 2 * p + 1):
                    k = act.activation(y[:, c, :], x[:, c, :], ACT.Identity, scale=col("gfin", c))
                k.then_inc(s_gained, 1)

            s0 = SLAB0["fdown"]
            behind(FT // 2 - 1)
            for s in range(s0 + 2, SLABS):
                split(s)
                for p in range(4):
                    if (44 * (p + 1) - 1) // 16 == s - 2 - s0:
                        act.wait_ge(s_drain["V"], DRAIN[GROUP0["fdown"] + p][1])
                        last_squares(p)
            act.wait_ge(s_drain["V"], DRAIN[GROUP0["fdown"] + 3][1])
            last_squares(3)
            keep_R(12, Rs[:, :])

        @block.vector
        def _(dve):
            chain = [0]

            def link(instruction):
                chain[0] += 1
                instruction.then_inc(s_dch, 1)
                dve.wait_ge(s_dch, chain[0])

            def split(b, i=None, turns=0, halves=(0, 1)):
                if i is None and b >= SLABS:
                    return
                for half in halves:
                    hs = slice(half * HALF, (half + 1) * HALF)
                    dve.wait_ge(s_hi, 2 * b + half + 1 if i is None else i * (2 * turns) + (2 * b + half + 1))
                    dve.tensor_tensor(wL[b % HL][:, hs], raw[b % RAW][:, hs], wH[b % HL][:, hs].bitcast(f32), ALU.subtract)\
                        .then_inc(s_lo, 1)

            def feed_pair(n, p, gain):
                for c in (2 * p, 2 * p + 1):
                    dve.wait_ge(s_xnH, C * n + c + 1)
                    k = dve.scalar_tensor_tensor(xnL[:, c, :], x[:, c, :], col(gain, c), xnH[:, c, :].bitcast(f32),
                                                 ALU.mult, ALU.subtract)
                k.then_inc(s_xn, 1)

            def mem_pair(p):
                for c in (2 * p, 2 * p + 1):
                    dve.wait_ge(s_mmH, c + 1)
                    k = dve.scalar_tensor_tensor(memL[:, c, :], mem[:, c, :], col("gmem", c), memH[:, c, :].bitcast(f32),
                                                 ALU.mult, ALU.subtract)
                k.then_inc(s_mm, 1)

            def mean_square(n):
                dve.wait_ge(s_sum, n + 1)
                dve.tensor_scalar(ms[:, :], pn[:, 0:TT], 1.0 / D, EPS, ALU.mult, ALU.add).then_inc(s_ms, 1)

            def diagonal(n):
                r = rmem if n == 1 else rtok
                dve.wait_ge(s_r, n + 1)
                for t in range(TT):
                    k = dve.tensor_scalar(diag[:, t, :], ident[:, :], r[:, t:t + 1], None, ALU.mult)
                k.then_inc(s_diag, 1)

            def group(name, i):
                dve.wait_ge(s_slab, SLAB0[name] + i + 1)
                return slot(GROUP0[name] + i)

            def keep(name, i, dst, R=None):
                psum = group(name, i)
                dve.tensor_tensor(dst, psum[:, :, 0:T], over_pair(Rs[:, :] if R is None else R), ALU.mult)\
                    .then_inc(s_drain["V"], 1)

            def mix_lo(src, pair, n):
                dve.wait_ge(s_mixH, n + 1)
                dve.tensor_tensor(mixL[:, 2 * pair:2 * pair + 2, :], src, mixH[:, 2 * pair:2 * pair + 2, :].bitcast(f32),
                                  ALU.subtract).then_inc(s_mix, 1)

            dve.memset(ones[:, :], 1.0)
            dve.memset(minus_half[:, :], -0.5)
            dve.memset(mrow[0][:, 0:P], 0.0)
            dve.memset(mrow[1][:, 0:P], 0.0)
            dve.memset(vx[:, :, :, VD:VD + 1], 1.0).then_inc(s_set, 1)

            dve.wait_ge(s_par, 16)
            feed_pair(0, 0, "g00")
            split(0, halves=(0,))
            feed_pair(0, 1, "g00")
            split(0, halves=(1,))
            feed_pair(0, 2, "g00")
            feed_pair(0, 3, "g00")
            split(1)
            mean_square(0)
            split(2, halves=(0,))
            dve.wait_ge(s_cst, 32)
            diagonal(0)
            dve.tensor_tensor(wgs[:, :, :], wg[:, :, :],
                              col("g00", 0, C).rearrange("p (c o) -> p c o", o=1).to_broadcast([P, C, 2 * NH]), ALU.mult)\
                .then_inc(s_wgs, 1)
            split(2, halves=(1,))
            dve.wait_ge(s_Rs, 1)
            keep("qk", 0, qT[:, 0:2, :])
            split(3)
            dve.wait_ge(s_gates, 1)
            for t in range(TT):
                k = dve.scalar_tensor_tensor(gz[:, t, :], pa[:, t * 8:t * 8 + 8], rtok[:, t:t + 1], col("bgates", 0, 2 * NH),
                                             ALU.mult, ALU.add)
            k.then_inc(s_gz, 1)
            keep("qk", 1, qT[:, 2:4, :])
            dve.wait_ge(s_gt, 1)
            dve.tensor_scalar(gcap[:, :, :], gt[:, :, :], CAP, None, ALU.mult).then_inc(s_gcap, 1)
            mem_pair(0)
            keep("qk", 2, kT[:, 0:2, :])
            split(4)
            dve.wait_ge(s_cum, 1)
            sums = pa[:, 0:TT * NH].rearrange("p (t h) -> p t h", t=TT)
            dve.tensor_copy(nb[:, :, :], sums)
            dve.wait_ge(s_gcap, 1)
            dve.tensor_tensor(av[:, :, :], gcap[:, :, 0:NH], sums, ALU.add).then_inc(s_av, 1)
            keep("qk", 3, kT[:, 2:4, :])
            split(5)
            dve.wait_ge(s_avT, 1)
            link(dve.tensor_scalar(mrow[0][:, P:], pb[0:NH, 0:T], 0.0, None, ALU.max))
            a, back = 0, 1
            while back < T:
                k = dve.tensor_tensor(mrow[1 - a][:, P:], mrow[a][:, P:], mrow[a][:, P - back:P - back + T], ALU.max)
                a, back = 1 - a, 2 * back
                if back < T:
                    link(k)
                else:
                    k.then_inc(s_mrow, 1)
            assert a == 0
            mem_pair(1)

            def exponents(h):
                dve.wait_ge(s_S, h + 1)
                if h:
                    dve.wait_ge(s_dexp, h)
                row = pn if h % 2 else pb
                dve.tensor_tensor(dargs[:, 0:T], maskt[:, :], row[:, 0:T], ALU.subtract)
                dve.tensor_tensor(dargs[:, T:T + P], maskt[:, 0:P], row[:, P:T], ALU.subtract).then_inc(s_darg, 1)

            def probabilities(h):
                dve.wait_ge(s_dexp, h + 1)
                dve.scalar_tensor_tensor(prob[h][:, :], (pc if h % 2 else pa)[:, 0:T + P], QK ** -0.5, dexp[:, :], ALU.mult, ALU.mult)\
                    .then_inc(s_P, 1)

            def normalise(h):
                dve.wait_ge(s_numk, h + 1)
                dve.wait_ge(s_em, 1)
                sums = num[h % 2][:, :, VD:VD + 1].rearrange("p t o -> p (t o)")
                link(dve.scalar_tensor_tensor(den[:, h, :], sums, -1.0, sums, ALU.mult, ALU.max))
                link(dve.tensor_tensor(den[:, h, :], den[:, h, :], em[:, :, h:h + 1].rearrange("p t o -> p (t o)"), ALU.max))
                link(dve.reciprocal(rec[:, h, :], den[:, h, :]))
                link(dve.tensor_tensor(rec2[:, h, :], rec[:, h, :], rec[:, h, :], ALU.mult))
                link(dve.scalar_tensor_tensor(hms[:, h, :], ssq[:, h, :], 1.0 / VD, rec2[:, h, :], ALU.mult, ALU.mult))
                dve.tensor_scalar(hms[:, h, :], hms[:, h, :], EPS, None, ALU.add).then_inc(s_hms, 1)
                dve.wait_ge(s_hr, h + 1)
                link(dve.tensor_tensor(hc[:, h, :], rec[:, h, :], hr[:, h, :], ALU.mult))
                if h >= 2:
                    dve.wait_ge(s_hT, h - 1)
                for t in range(TT):
                    k = dve.tensor_scalar(hn[h % 2][:, t, :], num[h % 2][:, t, 0:VD], hc[:, h, t:t + 1], None, ALU.mult)
                k.then_inc(s_hn, 1)

            def gated(h):
                dve.wait_ge(s_hT, h + 1)
                dve.wait_ge(s_osig, h + 1)
                if h:
                    dve.wait_ge(s_mix, h)
                for e in range(2):
                    k = dve.scalar_tensor_tensor(mixf[:, e, :], pn[:, e * T:(e + 1) * T], col("ghn", 2 * h + e),
                                                 sigo[:, 2 * h + e, :], ALU.mult, ALU.mult)
                k.then_inc(s_mixf, 1)

            def keep_o(i):
                keep("o", i, sigo[:, 2 * i:2 * i + 2, :])

            def fill_keys(h):
                dve.wait_ge(s_Rs, 2)
                keep(f"f{h}", 0, memk[:, 2 * h:2 * h + 2, :], Rm[:, :])

            split(6)
            dve.wait_ge(s_causal, 48)
            exponents(0)
            dve.wait_ge(s_mT, 1)
            dve.tensor_tensor(mdiff[:, :, :], nb[:, :, :], pn[:, 0:TT * NH].rearrange("p (t h) -> p t h", t=TT), ALU.subtract)\
                .then_inc(s_md, 1)
            probabilities(0)
            mem_pair(2)
            exponents(1)
            split(7)
            probabilities(1)
            mem_pair(3)
            exponents(2)
            split(8, halves=(0,))
            probabilities(2)
            split(8, halves=(1,))
            exponents(3)
            probabilities(3)
            mean_square(1)
            split(9)
            diagonal(1)
            normalise(0)
            keep_o(0)
            split(10, halves=(0,))
            normalise(1)
            gated(0)
            split(10, halves=(1,))
            mix_lo(mixf[:, :, :], 0, 0)
            normalise(2)
            keep_o(1)
            split(11, halves=(0,))
            gated(1)
            normalise(3)
            mix_lo(mixf[:, :, :], 1, 1)
            split(11, halves=(1,))
            keep_o(2)
            split(12, halves=(0,))
            gated(2)
            split(12, halves=(1,))
            mix_lo(mixf[:, :, :], 2, 2)
            keep_o(3)
            split(13, halves=(0,))
            gated(3)
            mix_lo(mixf[:, :, :], 3, 3)
            split(13, halves=(1,))

            def boundary(n, post, filler, feeds, gain, key):
                nxt = SLAB0[filler] + 1
                two = nxt == SLAB0[f"f{key}"]
                split(nxt, halves=(0,))
                mean_square(n)
                if two:
                    split(nxt, halves=(1,))
                    diagonal(n)
                    split(nxt + 1, halves=(0,))
                else:
                    diagonal(n)
                    split(nxt, halves=(1,))
                dve.wait_ge(s_R, n + 1)

                def scale(p):
                    ys = y[:, 2 * p:2 * p + 2, :]
                    dve.tensor_tensor(ys, ys, over_pair(pn[:, 128:128 + T]), ALU.mult).then_inc(s_t, 1)

                def add(p):
                    dve.wait_ge(s_t, 4 * post + p + 1)
                    xs, ys = x[:, 2 * p:2 * p + 2, :], y[:, 2 * p:2 * p + 2, :]
                    dve.tensor_tensor(xs, xs, ys, ALU.add).then_inc(s_xaddV, 1)

                scale(0)
                add(0)
                scale(1)
                scale(2)
                feed_pair(feeds, 0, gain)
                scale(3)
                add(2)
                if two:
                    split(nxt + 1, halves=(1,))
                for p in (1, 2, 3):
                    feed_pair(feeds, p, gain)
                fill_keys(key)
                split(nxt + 2 if two else nxt + 1)

            def out_phase(name):
                for i in range(3):
                    split(SLAB0[name] + i + 2)

            def norm_and_split(n, s):
                mean_square(n)
                split(s, halves=(0,))
                diagonal(n)
                split(s, halves=(1,))
                dve.wait_ge(s_Rs, kept_before(n)[0] + 1)

            def mlp(layer, n_norm):
                up, down = f"up{layer}", f"down{layer}"
                s0 = SLAB0[up]

                def hidden(n, i=None):
                    dve.wait_ge(s_hidH, 16 * layer + n + 1 if i is None else i * 4 + (16 * layer + n + 1))
                    hs = slice(2 * n, 2 * n + 2) if i is None else bass.ts(i * 4 + n, 2)
                    dve.tensor_tensor(hL[:, hs, :], hsq[n % 2][:, :, :], hH[:, hs, :].bitcast(f32), ALU.subtract)\
                        .then_inc(s_hid, 1)

                def relu(n, i=None):
                    dve.wait_ge(s_slab, s0 + n + 1 if i is None else i * 4 + (s0 + n + 1))
                    dve.scalar_tensor_tensor(hrelu[n % 2][:, :, :], slot(GROUP0[up] + n)[:, :, 0:T], 0.0, over_pair(Rs[:, :]),
                                             ALU.max, ALU.mult).then_inc(s_drain["V"], 1)

                norm_and_split(n_norm, s0 + 2)
                for n in range(4):
                    relu(n)
                    if n:
                        split(s0 + n + 2)
                    hidden(n)
                with dve.Fori(0, 3) as i:
                    for j in range(4):
                        relu(4 + j, i)
                        split(s0 + 4 + j + 2, i, 4)
                        hidden(4 + j, i)
                s0 = SLAB0[down]
                for kk in range(3):
                    split(s0 + kk + 2)
                with dve.Fori(0, 3) as i:
                    for kk in range(4):
                        split(s0 + 3 + kk + 2, i, 4)

            out_phase("out0")
            boundary(2, 0, "f4", 1, "g02", 0)
            mlp(0, 3)
            boundary(4, 1, "f1", 2, "g10", 1)

            c0 = SLAB0["cin"]
            norm_and_split(5, c0 + 2)
            dve.tensor_tensor(R2[:, :], Rs[:, :], Rs[:, :], ALU.mult)
            for e in range(2):
                k = dve.memset(upad[:, e, 0:2], 0.0)
            link(k)
            for i in range(12):
                j = i // 3
                if i % 3 == 1:
                    psum = group("cin", i)
                    dve.wait_ge(s_drain["A"], DRAIN[GROUP0["cin"] + i - 1][1])
                    if j:
                        dve.wait_ge(s_u, j)
                    dve.tensor_tensor(cx[:, :, :], psum[:, :, 0:T], csb[:, :, :], ALU.mult).then_inc(s_drain["V"], 1)
                    dve.wait_ge(s_drain["V"], DRAIN[GROUP0["cin"] + i][1])
                    dve.tensor_tensor(upad[:, :, 2:], cx[:, :, :], over_pair(R2[:, :]), ALU.mult).then_inc(s_u, 1)
                if i % 3 == 2:
                    if j:
                        dve.wait_ge(s_cf, j)
                    keep("cin", i, bsb[:, :, :])
                if i:
                    split(c0 + i + 2, halves=(0,) if i == 11 else (0, 1))
                if i % 3 == 1:
                    dve.wait_ge(s_cv, j + 1)
                    for tap in (1, 0):
                        for e in range(2):
                            k = dve.scalar_tensor_tensor(conv[:, e, :], upad[:, e, tap:tap + T], col("wconv", tap * C + 2 * j + e),
                                                         conv[:, e, :], ALU.mult, ALU.add)
                        link(k)
                if i % 3 == 2:
                    dve.wait_ge(s_drain["V"], DRAIN[GROUP0["cin"] + i][1])
                    if j:
                        dve.wait_ge(s_mix, 4 + j)
                    dve.tensor_tensor(cout[:, :, :], bsb[:, :, :], conv[:, :, :], ALU.mult).then_inc(s_cf, 1)
                    mix_lo(cout[:, :, :], j, 4 + j)
            split(c0 + 13, halves=(1,))
            out_phase("out1")
            boundary(6, 2, "f5", 3, "g12", 2)
            mlp(1, 7)
            boundary(8, 3, "f6", 4, "gmix", 3)

            for t in (upl[0][:, :, 0:PADW], upl[1][:, :, 0:PADW], sl[0][:, 0:PADW], sl[1][:, 0:PADW]):
                dve.memset(t, 0.0)
            r0 = SLAB0["rq"]
            norm_and_split(9, r0 + 2)
            for i in range(4):
                if i:
                    split(r0 + i + 2)
                dst = (rq if i < 2 else rk)[:, 2 * (i % 2):2 * (i % 2) + 2, :]
                keep("rq", i, dst)
                dve.wait_ge(s_drain["V"], DRAIN[GROUP0["rq"] + i][1])
                if i == 0:
                    dve.wait_ge(s_trigd, 2)
                else:
                    dve.wait_ge(s_rqk, i)
                dve.tensor_tensor(ropc[:, :, :], dst, over_pair(cost[:, :]), ALU.mult).then_inc(s_ropc, 1)

            def decayed(h):
                dve.wait_ge(s_rS, h + 1)
                dve.wait_ge(s_rc, 48)
                bank = pc if h % 2 else pa
                dve.tensor_tensor(rs[h][:, 0:T], bank[:, 0:T], decayt[:, h, :], ALU.mult)
                dve.tensor_tensor(rs[h][:, T:T + P], bank[:, T:T + P], decayt[:, h, 0:P], ALU.mult).then_inc(s_rs, 1)

            def ret_diagonal(h):
                if h >= 2:
                    dve.wait_ge(s_rR, h - 1)
                for t in range(TT):
                    k = dve.tensor_scalar(rdiag[h % 2][:, t, :], ident[:, :], rr8[:, h, t:t + 1], None, ALU.mult)
                k.then_inc(s_rdiag, 1)

            def ret_scaled(hp):
                bank = pc if hp else pa
                dve.wait_ge(s_rR, 2 * hp + 2)
                for e in range(2):
                    k = dve.scalar_tensor_tensor(ro[:, 2 * hp + e, :], ro[:, 2 * hp + e, :], col("gret", 2 * hp + e),
                                                 bank[:, e * T:(e + 1) * T], ALU.mult, ALU.mult)
                k.then_inc(s_rscaled, 1)

            def ret_out(hp):
                dve.wait_ge(s_rscaled, hp + 1)
                dve.wait_ge(s_rsg, hp + 1)
                if hp == 0:
                    dve.wait_ge(s_mix, 10)
                dve.tensor_tensor(ret_y[hp][:, :, :], ro[:, 2 * hp:2 * hp + 2, :], rsg[:, 2 * hp:2 * hp + 2, :], ALU.mult)\
                    .then_inc(s_ry, 1)

            u0 = SLAB0["ru"]
            split(u0 + 2)
            keep("ru", 0, upl[0][:, :, PADW:])
            split(u0 + 3, halves=(0,))
            decayed(0)
            split(u0 + 3, halves=(1,))
            decayed(1)
            keep("ru", 1, upl[1][:, :, PADW:])
            split(u0 + 4, halves=(0,))
            decayed(2)
            decayed(3)
            split(u0 + 4, halves=(1,))
            split(u0 + 5)
            split(u0 + 6, halves=(0,))
            mix_lo(yret[:, :, :], 0, 8)
            keep("rg", 0, rsg[:, 0:2, :])
            split(u0 + 6, halves=(1,))
            dve.wait_ge(s_rsum, 1)
            dve.tensor_scalar(rms8[:, :, :], pn[:, 0:NH * TT].rearrange("p (h t) -> p h t", h=NH), 1.0 / RH, EPS, ALU.mult,
                              ALU.add).then_inc(s_rms, 1)
            mix_lo(yret[:, :, :], 1, 9)
            dve.wait_ge(s_rr, 1)
            for h in range(NH):
                ret_diagonal(h)
            ret_scaled(0)
            ret_out(0)
            ret_scaled(1)
            keep("rg", 1, rsg[:, 2:4, :])
            mix_lo(ret_y[0][:, :, :], 2, 10)
            ret_out(1)
            mix_lo(ret_y[1][:, :, :], 3, 11)
            split(u0 + 7, halves=(0,))
            split(u0 + 7, halves=(1,))

            def residual(name, i):
                psum = group(name, i)
                dve.tensor_tensor(x[:, 2 * i:2 * i + 2, :], x[:, 2 * i:2 * i + 2, :], psum[:, :, 0:T], ALU.add)\
                    .then_inc(s_drain["V"], 1)

            for i in range(4):
                residual("out2", i)
                split(SLAB0["out2"] + i + 2)
                feed_pair(5, i, "gxa")

            def row_max(h):
                dve.wait_ge(s_xs, h + 1)
                bank = pn if h % 2 else pa
                for t in range(TT):
                    k = dve.reduce_max(xmax[:, h, t:t + 1], bank[:, t * T:(t + 1) * T], AX.X)
                link(k)
                dve.tensor_scalar(xneg[:, h, :], xmax[:, h, :], -(XH ** -0.5), None, ALU.mult).then_inc(s_xneg, 1)

            def row_norm(h):
                dve.wait_ge(s_xe, h + 1)
                link(dve.reciprocal(xrec[:, h, :], xsum[:, h, :]))
                if h >= 2:
                    dve.wait_ge(s_xT, h - 1)
                for t in range(TT):
                    k = dve.tensor_scalar(xpn[h % 2][:, t, :], xp[h % 2][:, t, :], xrec[:, h, t:t + 1], None, ALU.mult)
                k.then_inc(s_xpn, 1)

            def keep_query(h):
                psum = group("wq", h)
                if h >= 2:
                    dve.wait_ge(s_xs, h - 1)
                dve.tensor_tensor(xq[h % 2][:, :, :], psum[:, :, 0:T], over_pair(Rs[:, :]), ALU.mult).then_inc(s_drain["V"], 1)

            def xa_lo(h):
                mix_lo(pc[:, :].rearrange("p (a t) -> p a t", a=2), h, 12 + h)

            q0 = SLAB0["wq"]
            norm_and_split(10, q0 + 2)
            keep_query(0)
            keep_query(1)
            row_max(0)
            split(q0 + 3, halves=(0,))
            row_norm(0)
            row_max(1)
            split(q0 + 3, halves=(1,))
            row_norm(1)
            keep_query(2)
            split(q0 + 4)
            row_max(2)
            xa_lo(0)
            row_norm(2)
            keep_query(3)
            split(q0 + 5, halves=(0,))
            row_max(3)
            xa_lo(1)
            row_norm(3)
            split(q0 + 5, halves=(1,))
            xa_lo(2)
            split(q0 + 6)
            xa_lo(3)
            for i in range(4):
                residual("wo", i)
                split(SLAB0["wo"] + i + 2)
                feed_pair(6, i, "gffn")

            s0, d0 = SLAB0["fup"], DRAIN[GROUP0["fup"]][1]
            side = [cgate, cval]

            def scaled(n, i=None):
                def at(v):
                    return v if i is None else i * 4 + v
                dve.wait_ge(s_slab, at(s0 + n + 1))
                dve.tensor_tensor(apad[n % 2][:, :, 2:], slot(GROUP0["fup"] + n)[:, :, 0:T], over_pair(Rs[:, :]), ALU.mult)\
                    .then_inc(s_drain["V"], 1)

            def convolve(n, i=None):
                def at(v, m=4):
                    return v if i is None else i * m + v
                dve.wait_ge(s_fc, at(n + 1))
                for tap in (1, 0):
                    for e in range(2):
                        t = PCOL["fw"] + tap * FT + 2 * n + e
                        w = par[:, t:t + 1] if i is None else par[:, bass.ts(i * 8 + t, 1)]
                        c = side[n % 2][:, e, :]
                        k = dve.scalar_tensor_tensor(c, apad[n % 2][:, e, tap:tap + T], w, c, ALU.mult, ALU.add)
                    k.then_inc(s_fcd, 1)
                    if tap:
                        dve.wait_ge(s_fcd, at(2 * n + 1, 8))

            for a in apad:
                k = dve.memset(a[:, :, 0:2], 0.0)
            link(k)
            norm_and_split(11, s0 + 2)
            scaled(0)
            convolve(0)
            scaled(1)
            split(s0 + 3)
            convolve(1)
            with dve.Fori(0, (FT // 2 - 2) // 4) as i:
                for j in range(4):
                    scaled(2 + j, i)
                    split(s0 + 4 + j, i, 4)
                    convolve(2 + j, i)
            s0 = SLAB0["fdown"]
            for s in range(s0 + 2, SLABS + 2):
                split(s)
                for p in range(4):
                    if (44 * (p + 1) - 1) // 16 == s - 2 - s0:
                        dve.wait_ge(*group_done(p))
                        xs = x[:, 2 * p:2 * p + 2, :]
                        dve.tensor_tensor(xs, xs, slot(GROUP0["fdown"] + p)[:, :, 0:T], ALU.add).then_inc(s_drain["V"], 1)
            mean_square(12)
            diagonal(12)
            dve.wait_ge(s_Rs, kept_before(13)[0] + 1)
            for p in range(3):
                dve.wait_ge(s_gained, p + 1)
                ys = y[:, 2 * p:2 * p + 2, :]
                dve.tensor_tensor(ys, ys, over_pair(Rs[:, :]), ALU.mult).then_inc(s_outv, 1)

        @block.gpsimd
        def _(pool):
            chain = [0]

            def link(instruction):
                chain[0] += 1
                instruction.then_inc(s_pch, 1)
                pool.wait_ge(s_pch, chain[0])

            def add_squares(n):
                for p in (1, 2):
                    pool.wait_ge(s_sq, 4 * n + p + 1)
                    if p == 2:
                        pool.wait_ge(s_sqa, squares_added(n) + 1)
                    pool.tensor_tensor(sq[0], sq[0], sq[p], ALU.add).then_inc(s_sqa, 1)
                pool.wait_ge(s_sqa, squares_added(n) + 2)
                pool.tensor_tensor(sq[0][:, 0, :], sq[0][:, 0, :], sq[0][:, 1, :], ALU.add).then_inc(s_sqa, 1)
                if NORMS[n] == "pre":
                    pool.wait_ge(s_sq, 4 * n + 4)
                    for e in range(2):
                        pool.wait_ge(s_sqa, squares_added(n) + 3 + e)
                        pool.tensor_tensor(sq[0][:, 0, :], sq[0][:, 0, :], sq[3][:, e, :], ALU.add).then_inc(s_sqa, 1)

            def factor(n):
                r = rmem if n == 1 else rtok
                pool.wait_ge(s_ms, n + 1)
                pool.tensor_tensor(r[:, :], ms[:, :], minus_half[:, 0:TT], ALU.pow).then_inc(s_r, 1)

            def norm(n):
                add_squares(n)
                factor(n)

            def add_to_x(n):
                for p in (1, 3):
                    pool.wait_ge(s_t, 4 * n + p + 1)
                    xs = x[:, 2 * p:2 * p + 2, :]
                    pool.tensor_tensor(xs, xs, y[:, 2 * p:2 * p + 2, :], ALU.add).then_inc(s_xadd, 1)

            def angles():
                two_pi = 2 * math.pi
                big = 1.5 * 2.0 ** 23
                part1 = 6.28125
                part2 = 0.0019350051879882812
                part3 = two_pi - part1 - part2
                pool.wait_ge(s_sum, 8)
                pool.wait_ge(s_pos, 32)
                link(pool.tensor_copy(ang[:, :], posi[:, :]))
                link(pool.tensor_scalar(ang[:, :], ang[:, :], freqt[:, 0:1], None, ALU.mult))
                for turns in (0.25, 0.0):
                    whole = sint
                    link(pool.tensor_scalar(whole[:, :], ang[:, :], 1 / two_pi, turns, ALU.mult, ALU.add))
                    link(pool.tensor_scalar(whole[:, :], whole[:, :], big, None, ALU.add))
                    link(pool.tensor_scalar(whole[:, :], whole[:, :], big, None, ALU.subtract))
                    src, dst = ang, turn if turns else ang
                    for size in (part1, part2, part3):
                        link(pool.tensor_scalar(part[:, :], whole[:, :], size, None, ALU.mult))
                        link(pool.tensor_tensor(dst[:, :], src[:, :], part[:, :], ALU.subtract))
                        src = dst
                link(pool.tensor_scalar(turn[:, :], turn[:, :], math.pi / 2, 3.1415925, ALU.add, ALU.min))
                link(pool.tensor_scalar(turn[:, :], turn[:, :], -3.1415925, None, ALU.max))
                pool.tensor_scalar(ang[:, :], ang[:, :], 3.1415925, -3.1415925, ALU.min, ALU.max).then_inc(s_trig, 1)

            pool.wait_ge(s_set, 1)
            norm(0)
            norm(1)
            for h in range(NH):
                pool.wait_ge(s_hms, h + 1)
                pool.tensor_tensor(hr[:, h, :], hms[:, h, :], minus_half[:, 0:TT], ALU.pow).then_inc(s_hr, 1)
            for post in range(4):
                norm(2 + 2 * post)
                add_to_x(post)
                norm(3 + 2 * post)
                if post == 2:
                    angles()
            for i in range(4):
                dst = (rq if i < 2 else rk)[:, 2 * (i % 2):2 * (i % 2) + 2, :]
                pool.wait_ge(s_rot, i + 1)
                if i:
                    pool.wait_ge(s_rqk, i)
                pool.tensor_tensor(rops[:, :, :], rot[:, :, :], over_pair(sint[:, :]), ALU.mult).then_inc(s_rops, 1)
                pool.wait_ge(s_rops, i + 1)
                pool.wait_ge(s_ropc, i + 1)
                pool.tensor_tensor(dst, ropc[:, :, :], rops[:, :, :], ALU.add).then_inc(s_rqk, 1)
            pool.wait_ge(s_rqk, 4)
            for j in range(2):
                pool.wait_ge(s_drain["V"], DRAIN[GROUP0["ru"] + j][1])
                if j:
                    pool.wait_ge(s_pw, j)
                pool.wait_ge(s_rc, 48)
                for e in range(2):
                    w = WINDOWS[2 * j + e]
                    src, back, k = upl[j][:, e, :], 1, 0
                    while back < w:
                        link(pool.tensor_tensor(sl[k][:, PADW:], src[:, PADW:], src[:, PADW - back:PADW - back + T], ALU.add))
                        src, back, k = sl[k], 2 * back, 1 - k
                    pool.tensor_tensor(pooled[:, e, 0:16], src[:, PADW:PADW + 16], recountt[:, 2 * j + e, :], ALU.mult)
                    link(pool.tensor_scalar(pooled[:, e, 16:], src[:, PADW + 16:], 1.0 / w, None, ALU.mult))
                k = pool.tensor_tensor(pooled[:, :, :], pooled[:, :, :], upl[j][:, :, PADW:], ALU.subtract)
                k.then_inc(s_pool, 1)
            pool.wait_ge(s_rms, 1)
            pool.tensor_tensor(rr8[:, :, :].rearrange("p h t -> p (h t)"), rms8[:, :, :].rearrange("p h t -> p (h t)"),
                               minus_half[:, :], ALU.pow).then_inc(s_rr, 1)
            norm(10)
            norm(11)

            def product(m, i=None):
                def at(v, k=2):
                    return v if i is None else i * k + v
                hs = slice(2 * m, 2 * m + 2) if i is None else bass.ts(i * 2 + m, 2)
                pool.wait_ge(s_fs, at(m + 1))
                pool.wait_ge(s_fcd, at(4 * m + 4, 8))
                pool.tensor_tensor(cval[:, :, :], cgate[:, :, :], cval[:, :, :], ALU.mult).then_inc(s_fh, 1)
                pool.wait_ge(s_fH, at(m + 1))
                pool.tensor_tensor(hL[:, hs, :], cval[:, :, :], hH[:, hs, :].bitcast(f32), ALU.subtract).then_inc(s_f, 1)

            product(0)
            with pool.Fori(0, (FT // 4 - 1) // 2) as i:
                for j in range(2):
                    product(1 + j, i)
            norm(12)
            pool.wait_ge(s_Rs, kept_before(13)[0] + 1)
            pool.wait_ge(s_gained, 4)
            pool.tensor_tensor(y[:, 6:8, :], y[:, 6:8, :], over_pair(Rs[:, :]), ALU.mult).then_inc(s_outp, 1)


def _slabs(w, by=8):
    k, n = w.shape
    a = w.reshape(k // (by * P), by, P, n // 256, 256).transpose(3, 0, 2, 1, 4)
    return a.reshape(-1, P, SLAB)


def _stream(w):
    k, n = w.shape
    a = w.reshape(k // P, P, n // 256, 2, P).transpose(2, 0, 3, 1, 4).reshape(-1, 16, P, P)
    return a.transpose(0, 2, 1, 3).reshape(-1, P, SLAB)


def _lay_out(v):
    f = {k: np.asarray(a) for k, a in v.items()}
    cat = np.concatenate
    wi = f["w_in_mlstm"][0]
    q, k, vv, o, g = np.split(wi, [NH * QK, 2 * NH * QK, 2 * NH * QK + D, 2 * NH * QK + 2 * D], axis=1)
    fill_k, fill_v = _slabs(f["xa_wkv_2"][0][:, :D]), _slabs(f["xa_wkv_2"][0][:, D:])
    b, c, xh = (_slabs(a) for a in np.split(f["w_in_conv"][0], 3, axis=1))
    cin = np.stack([c, xh, b], axis=1).reshape(-1, P, SLAB)
    i2 = f["w_in_2"][0]
    rqk, rv, rg, ru = i2[:, :2 * RW], i2[:, 2 * RW:3 * RW], i2[:, 3 * RW:4 * RW], i2[:, 4 * RW:]
    wo2 = f["w_out_2"][0]
    gate, val = (_slabs(a) for a in np.split(f["ffn_w_up_2"][0], 2, axis=1))
    weights = cat([
        _slabs(q), _slabs(k), _slabs(vv), _slabs(o),
        _slabs(f["w_out_mlstm"][0]), fill_v[0:1], fill_k[0:1], _slabs(f["w_mlp_up"][0]), _slabs(f["w_mlp_down"][0]),
        fill_k[1:2], cin, _slabs(f["w_out_conv"][0]), fill_v[1:2], fill_k[2:3],
        _slabs(f["w_mlp_up"][1]), _slabs(f["w_mlp_down"][1]), fill_v[2:3], fill_k[3:4],
        _slabs(rqk), _slabs(ru), _slabs(rv), _slabs(rg),
        _slabs(cat([wo2[RW:], wo2[:RW]])), _slabs(f["xa_wq_2"][0]), fill_v[3:4], _slabs(f["xa_wo_2"][0]),
        np.stack([gate, val], axis=1).reshape(-1, P, SLAB), _stream(f["ffn_w_down_2"][0])])

    def cols(a):
        return a.reshape(-1, P).T

    def paired(a):
        return a.reshape(2, -1, 2, P).transpose(1, 0, 2, 3).reshape(-1, P).T

    ng = f["norm_g"]
    params = cat([cols(ng[i, j]) for i in range(2) for j in range(4)] + [
        cols(f["g_hnorm"][0]), cols(f["w_conv"][0]), cols(f["mix_norm_g_2"][0]), cols(f["ret_gn_g_2"][0]),
        cols(f["pool_scale_2"][0]), cols(f["xa_norm_g_2"][0]), cols(f["mem_norm_g_2"]), cols(f["ffn_norm_g_2"][0])]
        + [paired(f["ffn_conv_w_2"][0, i]) for i in range(3)] + [
        paired(f["ffn_conv_b_2"][0]), cols(f["final_norm_g_2"]), np.broadcast_to(f["b_gates_mlstm"][0], (P, 2 * NH))], axis=1)

    def chunks(a):
        return a.reshape(-1, P, a.shape[-1]).transpose(1, 0, 2)

    s, l = np.arange(P)[:, None], np.arange(T)[None, :]
    tri = np.stack([(s <= l[:, :P]).astype(np.float32), np.eye(P, dtype=np.float32)])
    mask = np.where(s <= l, 0.0, BLOCKED).astype(np.float32)
    select = np.zeros((NH, NH, P), np.float32)
    for h in range(NH):
        select[h, h] = 1.0
    lg = np.log1p(-np.exp2(-5.0 - np.arange(NH)))
    decay = np.where(s[:, None] <= l[None], np.exp(lg[None, :, None] * np.maximum(l[None] - s[:, None], 0)), 0.0) * RH ** -0.5
    half = np.arange(0, RH, 2, dtype=np.float32)
    freq = np.exp(np.float32(-math.log(ROPE_BASE)) * half / np.float32(RH)).astype(np.float32)
    freq = np.tile(freq, 2)[:, None]
    recount = np.stack([1.0 / np.minimum(np.arange(1, 17), w) for w in WINDOWS]).astype(np.float32)
    return {
        "xT": chunks(f["x"][0].T), "memT": chunks(f["mem_2"][0].T), "pos": f["positions_2"][0], "weights": weights,
        "wgate": chunks(g), "params": params, "poolw": f["pool_w_2"][0].transpose(1, 0, 2), "tri": tri, "mask": mask,
        "select": select, "decay": decay.astype(np.float32), "freq": freq,
        "recount": np.broadcast_to(recount, (P, NH, 16)),
    }


def kernel(**inputs):
    import concourse.bacc as bacc
    from concourse.bass_utils import run_bass_kernel_spmd

    nc = bacc.Bacc("TRN2", target_bir_lowering=False, num_devices=1)
    arrays, args = {}, []
    for name, a in _lay_out(inputs).items():
        a = np.ascontiguousarray(a)
        arrays[f"in_{name}"] = a
        args.append(nc.dram_tensor(f"in_{name}", a.shape, mybir.dt.from_np(a.dtype), kind="ExternalInput").ap())
    args.append(nc.dram_tensor("out", (P, C, T), mybir.dt.float32, kind="ExternalOutput").ap())
    build(nc, *args)
    result = run_bass_kernel_spmd(nc, [arrays], core_ids=[0]).results[0]["out"]
    return result.transpose(2, 1, 0).reshape(1, T, D)
```
